# Optimizing a Trainium2 kernel written in Bass

```python
import math
import jax
import jax.numpy as jnp
from jax import lax
import numpy as np

D_MODEL = 1024
BATCH = 1
SEQ = 256
DEPTH = 2

F32 = jnp.float32
GRID_W = 64
CTX_LEN = 256
N_MIXERS = 2
N_MLSTM_LAYERS = (DEPTH + 1) // 2
N_DIFF_LAYERS = DEPTH // 2
EPS = 1e-6

M_HEADS = 4
M_HEAD_DIM = D_MODEL // M_HEADS
M_CONV_W = 5
M_CHUNK = 64
M_GATES = 4 * M_HEADS
M_IN = 4 * D_MODEL + M_GATES

D_HEADS = 8
D_HEAD_DIM = D_MODEL // (2 * D_HEADS)
D_V_DIM = 2 * D_HEAD_DIM
D_IN = 3 * D_MODEL
Q_BLOCK = 128
ROPE_BASE = 10000.0
ROPE_FREQS = D_HEAD_DIM // 4

N_GROUPS = 4
EXPERTS_PER_GROUP = 8
N_EXPERTS = N_GROUPS * EXPERTS_PER_GROUP
TOP_K = 2
D_EXPERT = 512
MOE_BLOCK = 128

kernel_name = 'hybrid_mlstm_diffattn_hmoe'

def rmsnorm(x, g):
    xf = x.astype(F32)
    y = xf * lax.rsqrt(jnp.mean(xf * xf, axis=-1, keepdims=True) + EPS)
    return (y * g.astype(F32)).astype(x.dtype)

def modulate(h, shift, scale):
    return h * (1 + scale) + shift

def dwconv_centered(x, w, b):
    pad = M_CONV_W // 2
    y = lax.conv_general_dilated(x, w[:, None, :].astype(x.dtype), window_strides=(1,),
                                 padding=[(pad, pad)], dimension_numbers=('NWC', 'WIO', 'NWC'),
                                 feature_group_count=x.shape[-1])
    return y + b.astype(x.dtype)

def mlstm_scan(q, k, v, i_log, f_log, state):
    b_, h_, t_, dh = q.shape
    nc = t_ // M_CHUNK

    def chunks(a):
        return jnp.moveaxis(a.reshape(a.shape[:2] + (nc, M_CHUNK) + a.shape[3:]), 2, 0)

    tri = jnp.tril(jnp.ones((M_CHUNK, M_CHUNK), bool))

    def step(carry, xs):
        C, n, m = carry
        qc, kc, vc, ic, fc = xs
        bcum = jnp.cumsum(fc, axis=-1)
        dmat = jnp.where(tri, bcum[..., :, None] - bcum[..., None, :] + ic[..., None, :], -jnp.inf)
        m_inter = bcum + m[..., None]
        m_out = jnp.maximum(m_inter, dmat.max(-1))
        w_intra = jnp.exp(dmat - m_out[..., None])
        w_inter = jnp.exp(m_inter - m_out)
        s = jnp.einsum('bhld,bhsd->bhls', qc, kc) * w_intra
        num = w_inter[..., None] * jnp.einsum('bhvd,bhld->bhlv', C, qc) + jnp.einsum('bhls,bhsv->bhlv', s, vc)
        den = w_inter * jnp.einsum('bhd,bhld->bhl', n, qc) + s.sum(-1)
        hout = num / jnp.maximum(jnp.abs(den), jnp.exp(-m_out))[..., None]
        b_last = bcum[..., -1]
        g = b_last[..., None] - bcum + ic
        m_next = jnp.maximum(b_last + m, g.max(-1))
        decay = jnp.exp(b_last + m - m_next)
        wg = jnp.exp(g - m_next[..., None])
        C = decay[..., None, None] * C + jnp.einsum('bhlv,bhld->bhvd', wg[..., None] * vc, kc)
        n = decay[..., None] * n + jnp.einsum('bhl,bhld->bhd', wg, kc)
        return (C, n, m_next), hout

    state, hs = lax.scan(step, state, tuple(chunks(a) for a in (q, k, v, i_log, f_log)))
    return jnp.moveaxis(hs, 0, 2).reshape(b_, h_, t_, dh), state

def mlstm_project(h, w_in, conv_w, conv_b, gate_b):
    b_, t_, _ = h.shape
    p = h @ w_in
    qk_pre, v, o_pre, gates = jnp.split(p, [2 * D_MODEL, 3 * D_MODEL, 4 * D_MODEL], axis=-1)
    qk = jax.nn.silu(dwconv_centered(qk_pre, conv_w, conv_b))
    q, k = jnp.split(qk, 2, axis=-1)

    def to_heads(a):
        return a.reshape(b_, t_, M_HEADS, M_HEAD_DIM).transpose(0, 2, 1, 3).astype(F32)

    q, k, v = to_heads(q), to_heads(k) * (M_HEAD_DIM ** -0.5), to_heads(v)
    gates = (gates.astype(F32) + gate_b.astype(F32)).reshape(b_, t_, 4, M_HEADS).transpose(2, 0, 3, 1)
    fwd = (gates[0], jax.nn.log_sigmoid(gates[2]))
    bwd = (gates[1], jax.nn.log_sigmoid(gates[3]))
    return q, k, v, jax.nn.sigmoid(o_pre), fwd, bwd

def mlstm_mixer(h_ctx, h_lat, w_in, conv_w, conv_b, gate_b, out_g, w_out):
    qc, kc, vc, oc, gfc, gbc = mlstm_project(h_ctx, w_in, conv_w, conv_b, gate_b)
    ql, kl, vl, ol, gfl, gbl = mlstm_project(h_lat, w_in, conv_w, conv_b, gate_b)
    b_ = h_lat.shape[0]
    zero = (jnp.zeros((b_, M_HEADS, M_HEAD_DIM, M_HEAD_DIM), F32),
            jnp.zeros((b_, M_HEADS, M_HEAD_DIM), F32), jnp.zeros((b_, M_HEADS), F32))
    rc_f, st_f = mlstm_scan(qc, kc, vc, gfc[0], gfc[1], zero)
    rl_f, _ = mlstm_scan(ql, kl, vl, gfl[0], gfl[1], st_f)
    fl = lambda a: jnp.flip(a, axis=2)
    rc_b, st_b = mlstm_scan(fl(qc), fl(kc), fl(vc), fl(gbc[0]), fl(gbc[1]), zero)
    rl_b, _ = mlstm_scan(fl(ql), fl(kl), fl(vl), fl(gbl[0]), fl(gbl[1]), st_b)

    def finish(r, o):
        r = r * lax.rsqrt(jnp.mean(r * r, axis=-1, keepdims=True) + EPS)
        r = r.transpose(0, 2, 1, 3).reshape(o.shape) * out_g.astype(F32)
        return (o * r.astype(o.dtype)) @ w_out

    return finish(rc_f + fl(rc_b), oc), finish(rl_f + fl(rl_b), ol)

def axial_rope_tables(rows):
    row = jnp.repeat(jnp.arange(rows), GRID_W)
    col = jnp.tile(jnp.arange(GRID_W), rows)
    inv = ROPE_BASE ** (-jnp.arange(ROPE_FREQS, dtype=F32) / ROPE_FREQS)
    ang = jnp.stack([row, col], axis=-1).astype(F32)[..., None] * inv
    return jnp.cos(ang), jnp.sin(ang)

def apply_rope(x, cos, sin):
    xs = x.reshape(x.shape[:-1] + (2, 2, ROPE_FREQS)).astype(F32)
    x1, x2 = xs[..., 0, :], xs[..., 1, :]
    cb, sb = cos[:, None], sin[:, None]
    out = jnp.stack([x1 * cb - x2 * sb, x1 * sb + x2 * cb], axis=-2)
    return out.reshape(x.shape).astype(x.dtype)

def diff_project(h, w_in, q_g, k_g):
    b_, t_, _ = h.shape
    q, k, v = jnp.split(h @ w_in, 3, axis=-1)

    def qk_heads(a):
        return a.reshape(b_, t_, D_HEADS, 2, D_HEAD_DIM).transpose(0, 2, 1, 3, 4)

    q = rmsnorm(qk_heads(q), q_g)
    k = rmsnorm(qk_heads(k), k_g)
    v = v.reshape(b_, t_, D_HEADS, D_V_DIM).transpose(0, 2, 1, 3)
    return q, k, v

def diff_attend(q, k, v, lam):
    s = jnp.einsum('bhqmd,bhkmd->mbhqk', q, k).astype(F32)
    p = jax.nn.softmax(s, axis=-1)
    a = p[0] - lam * p[1]
    return jnp.einsum('bhqk,bhkv->bhqv', a.astype(v.dtype), v)

def diff_mixer(h_ctx, h_lat, rope_cs, w_in, q_g, k_g, lq1, lk1, lq2, lk2, sub_g, w_out, lambda_init, need_ctx):
    scale = D_HEAD_DIM ** -0.5
    qc, kc, vc = diff_project(h_ctx, w_in, q_g, k_g)
    ql, kl, vl = diff_project(h_lat, w_in, q_g, k_g)
    cos, sin = rope_cs
    ql = apply_rope(ql, cos, sin) * scale
    kl = apply_rope(kl, cos, sin)
    lam = (jnp.exp(jnp.sum(lq1.astype(F32) * lk1.astype(F32)))
           - jnp.exp(jnp.sum(lq2.astype(F32) * lk2.astype(F32))) + lambda_init)
    k_all = jnp.concatenate([kc, kl], axis=2)
    v_all = jnp.concatenate([vc, vl], axis=2)
    b_, h_, t_ = ql.shape[:3]
    nb = t_ // Q_BLOCK
    qb = jnp.moveaxis(ql.reshape(b_, h_, nb, Q_BLOCK, 2, D_HEAD_DIM), 2, 0)
    ol = lax.map(lambda qq: diff_attend(qq, k_all, v_all, lam), qb)
    ol = jnp.moveaxis(ol, 0, 2).reshape(b_, h_, t_, D_V_DIM)

    def finish(o):
        o = rmsnorm(o, sub_g) * (1.0 - lambda_init)
        return o.transpose(0, 2, 1, 3).reshape(o.shape[0], o.shape[2], D_MODEL) @ w_out

    yl = finish(ol)
    yc = finish(diff_attend(qc * scale, kc, vc, lam)) if need_ctx else None
    return yc, yl

def hier_moe(xt, grp_w, grp_b, exp_w, exp_b, w_gu, w_dn):
    n_tok = xt.shape[0]
    gprob = jax.nn.softmax((xt @ grp_w).astype(F32) + grp_b.astype(F32), axis=-1)
    gp_top, g_idx = lax.top_k(gprob, 1)
    elog = ((xt @ exp_w).astype(F32) + exp_b.astype(F32)).reshape(n_tok, N_GROUPS, EXPERTS_PER_GROUP)
    elog_g = elog[jnp.arange(n_tok), g_idx[:, 0]]
    e_val, e_idx = lax.top_k(elog_g, TOP_K)
    gate = (gp_top * jax.nn.softmax(e_val, axis=-1)).reshape(-1)
    eid = (g_idx * EXPERTS_PER_GROUP + e_idx).reshape(-1)
    tok = jnp.repeat(jnp.arange(n_tok, dtype=jnp.int32), TOP_K)
    n_assign = n_tok * TOP_K
    order = jnp.argsort(eid)
    e_s, t_s, g_s = eid[order], tok[order], gate[order]
    counts = jnp.bincount(eid, length=N_EXPERTS)
    padded = (counts + MOE_BLOCK - 1) // MOE_BLOCK * MOE_BLOCK
    pad_end = jnp.cumsum(padded)
    pad_start = pad_end - padded
    raw_start = jnp.cumsum(counts) - counts
    dest = pad_start[e_s] + jnp.arange(n_assign) - raw_start[e_s]
    cap = -(-n_assign // MOE_BLOCK) * MOE_BLOCK + N_EXPERTS * MOE_BLOCK
    nblk = cap // MOE_BLOCK
    tok_buf = jnp.zeros((cap,), jnp.int32).at[dest].set(t_s)
    gate_buf = jnp.zeros((cap,), F32).at[dest].set(g_s)
    blk_e = jnp.minimum(jnp.searchsorted(pad_end, jnp.arange(nblk) * MOE_BLOCK, side='right'), N_EXPERTS - 1)

    def expert_block(args):
        t_blk, e = args
        xb = xt[t_blk]
        g_, u_ = jnp.split(xb @ w_gu[e], 2, axis=-1)
        return (jax.nn.silu(g_) * u_) @ w_dn[e]

    y = lax.map(expert_block, (tok_buf.reshape(nblk, MOE_BLOCK), blk_e))
    y = y.reshape(cap, -1) * gate_buf[:, None].astype(y.dtype)
    return jax.ops.segment_sum(y, tok_buf, num_segments=n_tok)

def setup_inputs(seed: int = 0) -> dict:
    key = jax.random.key(seed)
    ks = jax.random.split(key, 32)
    nrm = lambda k, shape, s: s * jax.random.normal(k, shape, F32)
    d = D_MODEL
    f_bias = jnp.tile(jnp.linspace(3.0, 6.0, M_HEADS), 2)[None]
    return {
        'x': nrm(ks[0], (BATCH, SEQ, d), 1.0),
        'c': nrm(ks[1], (BATCH, d), 1.0),
        'ctx': nrm(ks[2], (BATCH, CTX_LEN, d), 1.0),
        'c_ctx': nrm(ks[3], (d,), 1.0),
        'ada_w': nrm(ks[4], (DEPTH, d, 6 * d), 0.5 * d ** -0.5),
        'ada_b': nrm(ks[5], (DEPTH, 6 * d), 0.02),
        'norm1_g': 1.0 + nrm(ks[6], (DEPTH, d), 0.1),
        'norm2_g': 1.0 + nrm(ks[7], (DEPTH, d), 0.1),
        'm_w_in': nrm(ks[8], (N_MLSTM_LAYERS, d, M_IN), d ** -0.5),
        'm_conv_w': nrm(ks[9], (N_MLSTM_LAYERS, M_CONV_W, 2 * d), M_CONV_W ** -0.5),
        'm_conv_b': nrm(ks[10], (N_MLSTM_LAYERS, 2 * d), 0.02),
        'm_gate_b': jnp.concatenate([nrm(ks[11], (N_MLSTM_LAYERS, 2 * M_HEADS), 0.1),
                                     f_bias + nrm(ks[12], (N_MLSTM_LAYERS, 2 * M_HEADS), 0.01)], axis=-1),
        'm_out_g': 1.0 + nrm(ks[13], (N_MLSTM_LAYERS, d), 0.1),
        'm_w_out': nrm(ks[14], (N_MLSTM_LAYERS, d, d), d ** -0.5),
        'd_w_in': nrm(ks[15], (N_DIFF_LAYERS, d, D_IN), d ** -0.5),
        'd_q_g': 1.0 + nrm(ks[16], (N_DIFF_LAYERS, D_HEAD_DIM), 0.1),
        'd_k_g': 1.0 + nrm(ks[17], (N_DIFF_LAYERS, D_HEAD_DIM), 0.1),
        'd_lq1': nrm(ks[18], (N_DIFF_LAYERS, D_HEAD_DIM), 0.1),
        'd_lk1': nrm(ks[19], (N_DIFF_LAYERS, D_HEAD_DIM), 0.1),
        'd_lq2': nrm(ks[20], (N_DIFF_LAYERS, D_HEAD_DIM), 0.1),
        'd_lk2': nrm(ks[21], (N_DIFF_LAYERS, D_HEAD_DIM), 0.1),
        'd_sub_g': 1.0 + nrm(ks[22], (N_DIFF_LAYERS, D_V_DIM), 0.1),
        'd_w_out': nrm(ks[23], (N_DIFF_LAYERS, d, d), d ** -0.5),
        'r_grp_w': nrm(ks[24], (DEPTH, d, N_GROUPS), d ** -0.5),
        'r_grp_b': nrm(ks[25], (DEPTH, N_GROUPS), 0.01),
        'r_exp_w': nrm(ks[26], (DEPTH, d, N_EXPERTS), d ** -0.5),
        'r_exp_b': nrm(ks[27], (DEPTH, N_EXPERTS), 0.01),
        'e_w_gu': nrm(ks[28], (DEPTH, N_EXPERTS, d, 2 * D_EXPERT), d ** -0.5),
        'e_w_dn': nrm(ks[29], (DEPTH, N_EXPERTS, D_EXPERT, d), D_EXPERT ** -0.5),
    }

def reference(x, c, ctx, c_ctx, ada_w, ada_b, norm1_g, norm2_g, m_w_in, m_conv_w, m_conv_b, m_gate_b,
              m_out_g, m_w_out, d_w_in, d_q_g, d_k_g, d_lq1, d_lk1, d_lq2, d_lk2, d_sub_g, d_w_out,
              r_grp_w, r_grp_b, r_exp_w, r_exp_b, e_w_gu, e_w_dn):
    b_, t_, d_ = x.shape
    rows = t_ // GRID_W
    rope_cs = axial_rope_tables(rows)
    sc = jax.nn.silu(c)
    scc = jax.nn.silu(c_ctx)
    xl, xc = x, ctx
    n_ctx = b_ * ctx.shape[1]
    for i in range(DEPTH):
        last = i == DEPTH - 1
        j = i // N_MIXERS
        mod = (sc @ ada_w[i] + ada_b[i]).reshape(b_, 6, 1, d_).transpose(1, 0, 2, 3)
        mod_c = (scc @ ada_w[i] + ada_b[i]).reshape(6, 1, 1, d_)
        hl = modulate(rmsnorm(xl, norm1_g[i]), mod[0], mod[1])
        hc = modulate(rmsnorm(xc, norm1_g[i]), mod_c[0], mod_c[1])
        if i % N_MIXERS == 0:
            yc, yl = mlstm_mixer(hc, hl, m_w_in[j], m_conv_w[j], m_conv_b[j], m_gate_b[j], m_out_g[j], m_w_out[j])
        else:
            yc, yl = diff_mixer(hc, hl, rope_cs, d_w_in[j], d_q_g[j], d_k_g[j], d_lq1[j], d_lk1[j], d_lq2[j],
                                d_lk2[j], d_sub_g[j], d_w_out[j], 0.8 - 0.6 * math.exp(-0.3 * i), not last)
        xl = xl + mod[2] * yl
        hl = modulate(rmsnorm(xl, norm2_g[i]), mod[3], mod[4]).reshape(-1, d_)
        if last:
            y = hier_moe(hl, r_grp_w[i], r_grp_b[i], r_exp_w[i], r_exp_b[i], e_w_gu[i], e_w_dn[i])
            xl = xl + mod[5] * y.reshape(b_, t_, d_)
        else:
            xc = xc + mod_c[2] * yc
            hc = modulate(rmsnorm(xc, norm2_g[i]), mod_c[3], mod_c[4]).reshape(-1, d_)
            y = hier_moe(jnp.concatenate([hc, hl], axis=0), r_grp_w[i], r_grp_b[i], r_exp_w[i], r_exp_b[i],
                         e_w_gu[i], e_w_dn[i])
            xc = xc + mod_c[5] * y[:n_ctx].reshape(xc.shape)
            xl = xl + mod[5] * y[n_ctx:].reshape(b_, t_, d_)
    return xl


_drawn_inputs = setup_inputs


def setup_inputs(seed=0):
    import zlib

    import numpy as np

    out = dict(_drawn_inputs(seed))
    spreads = {}
    factors = {'m_conv_b': 8.0,
     'd_q_g': 3.934,
     'd_k_g': 4.108,
     'd_lq2': 5.287,
     'd_lk2': 4.321,
     'd_sub_g': 2.981,
     'r_grp_b': 6.91,
     'r_exp_b': 5.373}
    for name, (base, spread) in spreads.items():
        noise = np.random.default_rng([zlib.crc32(name.encode()), seed]).standard_normal(out[name].shape)
        drawn = base * np.exp(spread * noise) if base else spread * noise
        out[name] = jnp.asarray(drawn.astype(out[name].dtype))
    for name, factor in factors.items():
        out[name] = (out[name] * factor).astype(out[name].dtype)
    return out
```

```python
import math
from contextlib import ExitStack

import concourse.bass as bass
from concourse import mybir
from concourse.alu_op_type import AluOpType as ALU

F32 = mybir.dt.float32
I32 = mybir.dt.int32
U32 = mybir.dt.uint32
ACT = mybir.ActivationFunctionType
AX_X = mybir.AxisListType.X

P = 128
D = 1024
KT = D // P
NCTX, NLAT = 256, 256
TOK = NCTX + NLAT
TILES = TOK // P
LAT = [2, 3]
ALL = [0, 1, 2, 3]
HALF = 512
EPS = 1e-6
NEG = -1e30

MH, MDH = 4, 256
TAPS = 5
DH, DDH, DDV = 8, 64, 128
LAMBDA_INIT = 0.8 - 0.6 * math.exp(-0.3)

NG, NPG = 4, 8
NE = NG * NPG
DE = 512
B = 32
NBMAX = TOK // B
TMAX = NE + 2 * TOK // B
XROWS = (TMAX + 1) * B

GU, DN = 8192, 4096
SLOT = GU + DN
WCH = 4096
W_AT = [2 * SLOT + WCH, 2 * SLOT + GU, 3 * SLOT, 0]
X_AT = 3 * SLOT + WCH
ARENA = X_AT + TILES * D
NW = len(W_AT)

STREAM = [("ada", 0, c) for c in range(4)]
_ada = [("ada", 0, c) for c in range(4, 12)] + [("ada", 1, c) for c in range(4)]
for _j in range(8):
    STREAM += [("m_in", _j)] + _ada[2 * _j:2 * _j + 2]
STREAM += [("m_out", 0), ("m_out", 1)]
_ada = [("ada", 1, c) for c in range(4, 12)]
for _j, _c in enumerate([2, 3, 0, 1, 4, 5]):
    STREAM += [("d_in", _c)] + _ada[2 * _j:2 * _j + 2]
STREAM += [("d_out", 0), ("d_out", 1)]
AT = {key: n for n, key in enumerate(STREAM)}
ADA = [n for n, key in enumerate(STREAM) if key[0] == "ada"]


class Chain:

    def __init__(self, sem):
        self.sem, self.n = sem, 0

    def link(self, eng, ins):
        ins.then_inc(self.sem, 1)
        self.n += 1
        eng.wait_ge(self.sem, self.n)


def bc(ap, shape):
    return ap.to_broadcast(shape)


def hybrid_backbone(nc, x, c, ctx, c_ctx, ada_w, ada_b, norm1_g, norm2_g, m_w_in, m_conv_w,
                    m_conv_b, m_gate_b, m_out_g, m_w_out, d_w_in, d_q_g, d_k_g, d_lq1, d_lk1,
                    d_lq2, d_lk2, d_sub_g, d_w_out, r_grp_w, r_grp_b, r_exp_w, r_exp_b,
                    e_w_gu, e_w_dn, rope, out, debug=None):
    stack = ExitStack()
    sb = lambda name, shape, dt=F32: stack.enter_context(nc.sbuf_tensor(name, shape, dt))
    own = []

    def sem(name):
        if not own:
            return stack.enter_context(nc.semaphore(name))
        own[-1].append(nc.alloc_semaphore(name=name))
        return own[-1][-1]

    def phase(build_phase):
        def built(*args):
            own.append([])
            build_phase(*args)
            multiplied.clear()
            nc.clear_and_free_semaphores(own.pop())
            nc.all_engine_barrier()
        return built


    arena = sb("arena", [P, ARENA])
    bank = [stack.enter_context(nc.psum_tensor(f"bank{i}", [P, HALF], F32)) for i in range(8)]

    def region(at, *shape):
        n = math.prod(shape)
        v = arena[:, at:at + n]
        if len(shape) == 2:
            v = v.rearrange("p (a b) -> p a b", a=shape[0])
        elif len(shape) == 3:
            v = v.rearrange("p (a b c) -> p a b c", a=shape[0], b=shape[1])
        return v

    gu_w = [region(s * SLOT, KT, D) for s in range(3)]
    dn_w = [region(s * SLOT + GU, DE // P, D) for s in range(3)]
    wch = [region(a, KT, HALF) for a in W_AT]
    X = region(X_AT, TILES, D)
    hT = region(2 * SLOT, KT, TOK)
    h2T = region(W_AT[2], KT, TOK)

    S1 = sb("S1", [P, 2, D])
    S2 = sb("S2", [P, 2, D + 16])
    MASK = sb("MASK", [P, 3, HALF])
    ident = sb("ident", [P, P])
    upto = sb("upto", [P, P])
    after = sb("after", [P, P])
    before = sb("before", [P, P])
    ones = sb("ones", [P, P])
    veca, vecb, vecc = (region(SLOT + i * P, P) for i in range(3))
    rowv = region(SLOT + 3 * P, HALF)[0:1, :]
    vT = sb("vT", [P, 3, P])
    modT = sb("modT", [P, 2, 6 * KT, 2])
    rw = sb("rw", [P, KT, 64])
    rowb = sb("rowb", [P, HALF])
    sc = sb("sc", [P, KT, 32])
    small = sb("small", [P, 896])
    eps = sb("eps", [P, 1])
    iot = sb("iot", [P, 96], I32)
    iof = sb("iof", [P, 96])
    tab = sb("tab", [1, 2 * NE + 1], I32)
    pos = sb("pos", [P, 2, TILES], I32)
    gat = sb("gat", [P, 2, TILES])

    xs = nc.dram_tensor("xs", (XROWS, D), F32, kind="Internal").ap()
    ys = nc.dram_tensor("ys", (XROWS, D), F32, kind="Internal").ap()
    tabd = nc.dram_tensor("tabd", (2, 2 * NE + 1), I32, kind="Internal").ap()

    G = S2[:, :, 0:D]
    MASK_ROW = MASK[:].rearrange("p a b -> p (a b)")[:, 0:D]
    GATE_B, GRP, QG, KG, LQ = 0, 16, 88, 152, 216
    NROW = LQ + 4 * DDH
    N1G, N2G, CONVB, CONVW = 0, 16, 32, 48
    OUTG, CVEC, CCTX, SUBG = 0, 8, 16, 24

    w_loaded = [sem(f"w_loaded{s}") for s in range(NW)]
    multiplied = {}
    gu_loaded = [[sem(f"gu_loaded{s}_{b}") for b in range(2)] for s in range(3)]
    dn_loaded = [[sem(f"dn_loaded{s}_{b}") for b in range(2)] for s in range(3)]
    rw_loaded = sem("rw_loaded")

    WSRC = {"m_in": m_w_in[0], "m_out": m_w_out[0], "d_in": d_w_in[0], "d_out": d_w_out[0]}

    def load_chunk(eng, n):
        kind, *at = STREAM[n]
        src = ada_w[at[0]] if kind == "ada" else WSRC[kind]
        src = src[:, at[-1] * HALF:(at[-1] + 1) * HALF].rearrange("(k p) n -> p k n", p=P)
        if n - NW in ADA:
            eng.wait_ge(ada_mm, ADA.index(n - NW) + 1)
        elif n - NW in multiplied:
            eng.wait_ge(*multiplied[n - NW])
        eng.dma_start(wch[n % NW], src).then_inc(w_loaded[n % NW], 16)

    def chunk(eng, n):
        eng.wait_ge(w_loaded[n % NW], 16 * (n // NW + 1))
        return wch[n % NW]

    def load_rw(eng, layer):
        with nc.allow_non_contiguous_dma(reason="narrow router weights"):
            eng.dma_start(rw[:, :, 0:NG], r_grp_w[layer].rearrange("(k p) n -> p k n", p=P)).then_inc(rw_loaded, 16)
            eng.dma_start(rw[:, :, NG:NG + NE], r_exp_w[layer].rearrange("(k p) n -> p k n", p=P)).then_inc(rw_loaded, 16)

    ada_mm, ada_cp, ada_tr, ada_part, ada_out = (sem(f"ada_{n}") for n in ("mm", "copied", "turned", "half", "out"))
    adas = small[:, 384:896].rearrange("p (b n) -> p b n", b=2)

    def ada_multiply(pe, n):
        i = ADA.index(n)
        w = chunk(pe, n)
        if i:
            pe.wait_ge(ada_cp, i)
        for k in range(0, KT, 2):
            for q in range(4):
                kk, hf = k + q // 2, q % 2
                last = pe.matmul(bank[6][32 * q:32 * q + 32, 0:256], sc[:, kk, :], w[:, kk, hf * 256:(hf + 1) * 256],
                                 start=(k == 0), stop=(k == KT - 2), skip_group_check=True)
        last.then_inc(ada_mm, 1)

    def ada_turn(pe, n):
        i = ADA.index(n)
        pe.wait_ge(ada_cp, i + 1)
        if i:
            pe.wait_ge(ada_out, i)
        for j in range(2):
            last = pe.transpose(bank[7][:, j * P:(j + 1) * P], adas[:, i % 2, j * P:(j + 1) * P], ident[:])
        last.then_inc(ada_tr, 1)

    def ada_copy(dve, n):
        i = ADA.index(n)
        dve.wait_ge(ada_mm, i + 1)
        if i >= 2:
            dve.wait_ge(ada_tr, i - 1)
        dve.tensor_copy(adas[:, i % 2, :], bank[6][:, 0:256]).then_inc(ada_cp, 1)

    def ada_finish(dve, n):
        i = ADA.index(n)
        _, layer, ci = STREAM[n]
        dve.wait_ge(ada_tr, i + 1)
        turned = bank[7][:, 0:256].rearrange("p (j a h s) -> p a j h s", j=2, a=2, h=2)
        cols = slice(ci * 4, ci * 4 + 4)
        to = modT[:, layer, cols, :].rearrange("p (h j) s -> p j h s", h=2)
        bias = vT[:, 0, layer * 48 + ci * 4:layer * 48 + ci * 4 + 4].rearrange("p (h j) -> p j h", h=2).unsqueeze(3)
        dve.tensor_tensor(to, turned[:, 0, :, :, 0:2], bc(bias, [P, 2, 2, 2]), ALU.add).then_inc(ada_part, 1)
        dve.wait_ge(ada_part, i + 1)
        dve.tensor_tensor(to, to, turned[:, 1, :, :, 0:2], ALU.add).then_inc(ada_out, 1)

    row_ss, row_std, row_rstd = small[:, 16:20], small[:, 20:24], small[:, 24:28]

    def row_squares(act, i, t, junk, squares):
        if i:
            act.wait_ge(squares, i)
        act.activation(junk, X[:, t, :], ACT.Square, accum_out=row_ss[:, i:i + 1]).then_inc(squares, 1)

    def row_roots(act, nt, squares, std):
        act.wait_ge(squares, nt)
        act.activation(row_std[:, 0:nt], row_ss[:, 0:nt], ACT.Sqrt, bias=eps[:], scale=1.0 / D).then_inc(std, 1)

    def row_inverses(dve, nt, std):
        dve.wait_ge(std, 1)
        dve.reciprocal(row_rstd[:, 0:nt], row_std[:, 0:nt]).then_inc(std, 1)

    @phase
    def setup():
        vec, rowl, xl, const, vt_t, vt_r, rb, scr = (sem(f"setup_{n}") for n in (
            "vec", "row", "x", "const", "turned", "columns", "rows", "silu"))
        squares, std = sem("setup_squares"), sem("setup_std")
        rows = [(GATE_B, m_gate_b)]
        for layer in range(2):
            rows += [(GRP + 36 * layer, r_grp_b[layer:layer + 1, :]), (GRP + 36 * layer + NG, r_exp_b[layer:layer + 1, :])]
        rows += [(QG, d_q_g), (KG, d_k_g), (LQ, d_lq1), (LQ + DDH, d_lk1), (LQ + 2 * DDH, d_lq2), (LQ + 3 * DDH, d_lk2)]
        with nc.Block() as block:
            @block.sync
            def _(sp):
                sp.dma_start(vecc[0:8, :], m_out_g[0].rearrange("(r p) -> r p", p=P)).then_inc(vec, 16)
                sp.dma_start(vecc[8:16, :], c[0].rearrange("(r p) -> r p", p=P)).then_inc(vec, 16)
                sp.dma_start(vecc[16:24, :], c_ctx.rearrange("(r p) -> r p", p=P)).then_inc(vec, 16)
                sp.dma_start(vecc[24:25, :], d_sub_g).then_inc(vec, 16)
                sp.dma_start(veca[0:96, :], ada_b.rearrange("l (r p) -> (l r) p", p=P)).then_inc(vec, 16)
                sp.dma_start(X[:, 0:2, :], ctx[0].rearrange("(t p) d -> p t d", p=P)).then_inc(xl, 16)
                sp.dma_start(X[:, 2:4, :], x[0].rearrange("(t p) d -> p t d", p=P)).then_inc(xl, 16)
                for n in range(4 + NW):
                    load_chunk(sp, n)

            @block.scalar
            def _(act):
                act.dma_start(vecb[0:16, :], norm1_g.rearrange("l (r p) -> (l r) p", p=P)).then_inc(vec, 16)
                act.dma_start(vecb[16:32, :], norm2_g.rearrange("l (r p) -> (l r) p", p=P)).then_inc(vec, 16)
                act.dma_start(vecb[32:48, :], m_conv_b[0].rearrange("(r p) -> r p", p=P)).then_inc(vec, 16)
                act.dma_start(vecb[48:128, :], m_conv_w[0].rearrange("j (r p) -> (j r) p", p=P)).then_inc(vec, 16)
                for at, src in rows:
                    act.dma_start(rowv[0:1, at:at + src.shape[1]], src).then_inc(rowl, 16)
                act.wait_ge(vt_r, 3)
                act.activation(sc[:, :, 0], vT[:, 2, CCTX:CCTX + KT], ACT.Silu).then_inc(scr, 1)
                act.activation(sc[:, :, 1], vT[:, 2, CVEC:CVEC + KT], ACT.Silu).then_inc(scr, 1)
                act.wait_ge(scr, 3)
                act.wait_ge(xl, 32)
                for t in ALL:
                    row_squares(act, t, t, S2[:, 0, 0:D], squares)
                row_roots(act, TILES, squares, std)

            @block.gpsimd
            def _(pool):
                pool.memset(ones[:], 1.0).then_inc(const, 1)
                pool.memset(MASK[:], 0.0).then_inc(const, 1)
                pool.wait_ge(const, 2)
                sel = lambda o, i, op, cm, st, fill: pool.affine_select(
                    out=o, in_=i, compare_op=op, fill=fill, base=0, pattern=[[st, P]], channel_multiplier=cm)
                sel(ident[:], ones[:], ALU.is_equal, 1, -1, 0.0).then_inc(const, 1)
                sel(upto[:], ones[:], ALU.is_ge, -1, 1, 0.0).then_inc(const, 1)
                sel(after[:], ones[:], ALU.is_ge, 1, -1, 0.0).then_inc(const, 1)
                sel(before[:], ones[:], ALU.is_gt, -1, 1, 0.0).then_inc(const, 1)
                sel(MASK[:, 0, 3 * P:4 * P], MASK[:, 0, 3 * P:4 * P], ALU.is_ge, 1, -1, NEG).then_inc(const, 1)
                sel(MASK[:, 1, 2 * P:3 * P], MASK[:, 1, 2 * P:3 * P], ALU.is_ge, -1, 1, NEG).then_inc(const, 1)
                sel(MASK[:, 2, 3 * P:4 * P], MASK[:, 2, 3 * P:4 * P], ALU.is_ge, -1, 1, NEG).then_inc(const, 1)
                pool.memset(MASK[:, 2, 2 * P:3 * P], NEG).then_inc(const, 1)
                pool.iota(iot[:, 0:NE], pattern=[[-1, NE]], base=NE, channel_multiplier=0).then_inc(const, 1)
                pool.iota(iot[:, NE:NE + NBMAX], pattern=[[B, NBMAX]], base=B, channel_multiplier=0).then_inc(const, 1)

            @block.vector
            def _(dve):
                dve.memset(eps[:], EPS).then_inc(scr, 1)
                dve.memset(sc[:], 0.0).then_inc(scr, 1)
                dve.memset(rw[:], 0.0).then_inc(scr, 1)
                dve.wait_ge(const, 12)
                dve.tensor_copy(iof[:, 0:NE + NBMAX], iot[:, 0:NE + NBMAX]).then_inc(scr, 1)
                dve.wait_ge(scr, 4)
                dve.wait_ge(vt_t, 3)
                dve.tensor_copy(vT[:, 0, 0:96], bank[0][:, 0:96]).then_inc(vt_r, 1)
                dve.tensor_copy(vT[:, 1, :], bank[0][:, 128:256]).then_inc(vt_r, 1)
                dve.tensor_copy(vT[:, 2, 0:25], bank[0][:, 256:281]).then_inc(vt_r, 1)
                for n in range(4):
                    ada_copy(dve, n)
                    if n:
                        ada_finish(dve, n - 1)
                    if n == 2:
                        row_inverses(dve, TILES, std)
                ada_finish(dve, 3)
                dve.wait_ge(vt_t, 4)
                dve.tensor_copy(rowb[:, 0:NROW], bank[1][:, 0:NROW]).then_inc(rb, 1)

            @block.tensor
            def _(pe):
                pe.wait_ge(const, 3)
                pe.wait_ge(vec, 16 * 9)
                pe.transpose(bank[0][:, 0:96], veca[0:96, :], ident[0:96, 0:96]).then_inc(vt_t, 1)
                pe.transpose(bank[0][:, 128:256], vecb[:], ident[:]).then_inc(vt_t, 1)
                pe.transpose(bank[0][:, 256:281], vecc[0:25, :], ident[0:25, 0:25]).then_inc(vt_t, 1)
                pe.wait_ge(scr, 6)
                for n in range(4):
                    ada_multiply(pe, n)
                    if n:
                        ada_turn(pe, n - 1)
                ada_turn(pe, 3)
                pe.wait_ge(rowl, 16 * len(rows))
                pe.matmul(bank[1][:, 0:NROW], ones[0:1, :], rowv[0:1, 0:NROW], start=True, stop=True).then_inc(vt_t, 1)

    @phase
    def norm(layer, which, tiles, dst, extra_sync=None):
        g = vT[:, 1, (N1G, N2G)[which] + KT * layer:(N1G, N2G)[which] + KT * (layer + 1)].unsqueeze(2)
        shift = modT[:, layer, 24 * which:24 * which + KT, :]
        scale = modT[:, layer, 24 * which + KT:24 * which + 2 * KT, :]
        A = small[:, 0:16].rearrange("p (k s) -> p k s", k=KT)
        nt = len(tiles)
        a_, xn, tr, ev = (sem(f"norm{layer}{which}_{n}") for n in ("scale", "rows", "turned", "out"))
        with nc.Block() as block:
            @block.sync
            def _(sp):
                if extra_sync:
                    extra_sync(sp)

            @block.scalar
            def _(act):
                act.wait_ge(a_, 1)
                for si in range(nt // 2):
                    s = tiles[2 * si] // 2
                    for k in (2, 3, 6, 7):
                        act.wait_ge(tr, KT * si + 2 * (k // 2) + 2)
                        act.activation(dst[:, k, 256 * s:256 * s + 256], bank[4 * si + k // 2][:, 256 * (k % 2):256 * (k % 2) + 256], ACT.Identity,
                                       bias=shift[:, k, s:s + 1], scale=A[:, k, s:s + 1]).then_inc(ev, 1)

            @block.vector
            def _(dve):
                dve.scalar_tensor_tensor(out=A, in0=scale, scalar=1.0, in1=bc(g, [P, KT, 2]), op0=ALU.add,
                                         op1=ALU.mult).then_inc(a_, 1)
                dve.wait_ge(a_, 1)
                for si in range(nt // 2):
                    s = tiles[2 * si] // 2
                    if si:
                        dve.wait_ge(tr, KT * si)
                    for j in range(2):
                        i = 2 * si + j
                        dve.tensor_scalar(S1[:, j, :], X[:, tiles[i], :], row_rstd[:, i:i + 1], None, ALU.mult).then_inc(xn, 1)
                    for k in (0, 1, 4, 5):
                        dve.wait_ge(tr, KT * si + 2 * (k // 2) + 2)
                        dve.tensor_scalar(dst[:, k, 256 * s:256 * s + 256], bank[4 * si + k // 2][:, 256 * (k % 2):256 * (k % 2) + 256],
                                          A[:, k, s:s + 1], shift[:, k, s:s + 1], ALU.mult, ALU.add).then_inc(ev, 1)

            @block.tensor
            def _(pe):
                for si in range(nt // 2):
                    pe.wait_ge(xn, 2 * si + 2)
                    for k in range(KT):
                        for j in range(2):
                            last = pe.transpose(bank[4 * si + k // 2][:, (k % 2) * 256 + j * P:(k % 2) * 256 + (j + 1) * P],
                                                S1[:, j, k * P:(k + 1) * P], ident[:])
                        last.then_inc(tr, 1)

    qkT = region(SLOT, 2 * KT, TOK)
    V = region(SLOT + GU, TILES, D)
    O = region(GU, TILES, D)
    Fg = small[:, 32:64].rearrange("p (t c) -> p t c", t=TILES)
    ag = small[:, 64:96].rearrange("p (t c) -> p t c", t=TILES)

    @phase
    def mlstm_project():
        pad = S2[:, 0, :].rearrange("p (n) -> p n")
        padv = [S2[:, b, 0:520].rearrange("p (s n) -> p s n", s=2) for b in range(2)]
        accv = [S2[:, b, 520:520 + 512].rearrange("p (s n) -> p s n", s=2) for b in range(2)]
        lf = small[:, 96:128].rearrange("p (t c) -> p t c", t=TILES)
        g16 = small[:, 128:192].rearrange("p (t c) -> p t c", t=TILES)
        af, ex, ln = (small[:, a:a + 32].rearrange("p (t c) -> p t c", t=TILES) for a in (192, 224, 256))
        fu = small[:, 288:384].rearrange("p (w t c) -> p w t c", w=3, t=TILES)
        gmm, gdv, gac, fmm, done = (sem(f"gates_{n}") for n in ("mm", "vector", "scalar", "sums", "done"))
        unit, ev, padz, cv, si_, chain = (sem(f"mproj_{n}") for n in ("unit", "evacuated", "pads", "conv", "silu", "chain"))
        wg = sem("mproj_gate_w")
        NU = 32
        multiplied.update({AT[("m_in", j)]: (unit, 4 * (j + 1)) for j in range(NU // 4)})
        plan = []
        for j in range(8):
            n = AT[("m_in", j)]
            ada = [m for m in (n + 1, n + 2) if STREAM[m][0] == "ada"]
            first = 4 - len(ada)
            plan += [("unit", 4 * j + z) for z in range(first)]
            for z, m in enumerate(ada):
                plan += [("mul", m), ("unit", 4 * j + first + z), ("turn", m)]

        with nc.Block() as block:
            @block.sync
            def _(sp):
                with nc.allow_non_contiguous_dma(reason="narrow gate weights"):
                    sp.dma_start(rw[:, :, 0:16], m_w_in[0][:, 4 * D:4 * D + 16].rearrange("(k p) n -> p k n", p=P)).then_inc(wg, 16)
                for n in range(4 + NW, AT[("m_out", 1)] + 1):
                    load_chunk(sp, n)

            @block.tensor
            def _(pe):
                pe.wait_ge(wg, 16)
                for t in ALL:
                    for k in range(KT):
                        last = pe.matmul(bank[3][:, 64 * t:64 * t + 64], hT[:, k, t * P:(t + 1) * P], rw[:, k, :],
                                         start=(k == 0), stop=(k == KT - 1))
                last.then_inc(gmm, 1)

                def one(u):
                    j, z = u // 4, u % 4
                    w = chunk(pe, AT[("m_in", j)])
                    b = bank[u % 3]
                    if u >= 3:
                        pe.wait_ge(ev, u - 2)
                    for k in range(KT):
                        if j < 4:
                            last = pe.matmul(b[:], w[:, k, z * P:(z + 1) * P], hT[:, k, :], start=(k == 0), stop=(k == KT - 1))
                        else:
                            last = pe.matmul(b[:], hT[:, k, z * P:(z + 1) * P], w[:, k, :], start=(k == 0), stop=(k == KT - 1))
                    last.then_inc(unit, 1)

                for what, n in plan:
                    if what == "unit":
                        one(n)
                        if n == 1:
                            pe.wait_ge(done, 1)
                            flat = small[:, 96:128]
                            pe.matmul(bank[4][:, 0:32], upto[:], flat, start=True, stop=True)
                            pe.matmul(bank[4][:, 32:64], after[:], flat, start=True, stop=True)
                            pe.matmul(bank[4][:, 64:96], ones[:], flat, start=True, stop=True).then_inc(fmm, 1)
                    elif what == "mul":
                        ada_multiply(pe, n)
                    else:
                        ada_turn(pe, n)

            @block.scalar
            def _(act):
                act.wait_ge(gdv, 2)
                act.activation(ex, af, ACT.Exp, scale=-1.0).then_inc(gac, 1)
                act.wait_ge(gac, 1)
                act.activation(ln, ex, ACT.Ln, bias=1.0).then_inc(gac, 1)
                act.wait_ge(padz, 2)

                def silu(m):
                    act.wait_ge(cv, m + 1)
                    act.activation(qkT[:, m, :], accv[m % 2], ACT.Silu).then_inc(si_, 1)

                for u in range(NU):
                    act.wait_ge(unit, u + 1)
                    if u < 16:
                        if u >= 2:
                            act.wait_ge(cv, u - 1)
                        act.activation(padv[u % 2][:, :, 2:258], bank[u % 3][:].rearrange("p (s n) -> p s n", s=2), ACT.Copy).then_inc(ev, 1)
                        if u >= 1:
                            silu(u - 1)
                    elif u < 24:
                        if u == 16:
                            silu(15)
                        j, z = u // 4 - 4, u % 4
                        act.activation(V[:, z, j * HALF:(j + 1) * HALF], bank[u % 3][:], ACT.Copy).then_inc(ev, 1)
                    else:
                        j, z = u // 4 - 6, u % 4
                        act.activation(O[:, z, j * HALF:(j + 1) * HALF], bank[u % 3][:], ACT.Sigmoid).then_inc(ev, 1)

            @block.vector
            def _(dve):
                ch = Chain(chain)
                dve.memset(padv[0], 0.0).then_inc(padz, 1)
                dve.memset(padv[1], 0.0).then_inc(padz, 1)
                dve.wait_ge(gmm, 1)
                gp = bank[3][:, 0:256].rearrange("p (t n) -> p t n", t=TILES)
                dve.tensor_tensor(g16, gp[:, :, 0:16], bc(rowb[:, GATE_B:GATE_B + 16].unsqueeze(1), [P, TILES, 16]), ALU.add).then_inc(gdv, 1)
                dve.wait_ge(gdv, 1)
                f = g16[:, :, 8:16]
                dve.scalar_tensor_tensor(out=af, in0=f, scalar=-1.0, in1=f, op0=ALU.mult, op1=ALU.max).then_inc(gdv, 1)
                dve.wait_ge(gac, 2)
                dve.scalar_tensor_tensor(out=lf, in0=f, scalar=0.0, in1=ln, op0=ALU.min, op1=ALU.subtract).then_inc(done, 1)

                def sums():
                    dve.wait_ge(fmm, 1)
                    ch.link(dve, dve.tensor_copy(small[:, 288:384], bank[4][:, 0:96]))
                    tot = lambda t, a: fu[:, 2, t, a:a + 4]
                    for t in ALL:
                        ch.link(dve, dve.tensor_copy(Fg[:, t, 0:4], fu[:, 0, t, 0:4]))
                        ch.link(dve, dve.tensor_copy(Fg[:, t, 4:8], fu[:, 1, t, 4:8]))
                    earlier = {0: [0], 1: [], 2: [0, 1, 3], 3: [0, 1]}
                    earlier[0] = [1]
                    for t in ALL:
                        for o in range(t):
                            ch.link(dve, dve.tensor_tensor(Fg[:, t, 0:4], Fg[:, t, 0:4], tot(o, 0), ALU.add))
                        for o in earlier[t]:
                            ch.link(dve, dve.tensor_tensor(Fg[:, t, 4:8], Fg[:, t, 4:8], tot(o, 4), ALU.add))
                    ch.link(dve, dve.tensor_tensor(ag, g16[:, :, 0:8], Fg, ALU.subtract))

                def conv(m):
                    pd, ac = padv[m % 2], accv[m % 2]
                    col = lambda j: vT[:, 1, CONVW + j * 16 + m:CONVW + j * 16 + m + 1]
                    dve.wait_ge(ev, m + 1)
                    if m >= 2:
                        dve.wait_ge(si_, m - 1)
                    ch.link(dve, dve.tensor_scalar(ac, pd[:, :, 2:258], col(2), vT[:, 1, CONVB + m:CONVB + m + 1], ALU.mult, ALU.add))
                    for j in (0, 1, 3):
                        ch.link(dve, dve.scalar_tensor_tensor(out=ac, in0=pd[:, :, j:j + 256], scalar=col(j), in1=ac, op0=ALU.mult, op1=ALU.add))
                    dve.scalar_tensor_tensor(out=ac, in0=pd[:, :, 4:260], scalar=col(4), in1=ac, op0=ALU.mult, op1=ALU.add).then_inc(cv, 1)

                dve.wait_ge(padz, 2)
                for what, n in plan:
                    if what == "unit":
                        if n < 16:
                            conv(n)
                        if n == 2:
                            sums()
                    elif what == "mul":
                        ada_copy(dve, n)
                    else:
                        ada_finish(dve, n)

    SEEN = {(0, 0): (0, 1), (1, 0): (0, 2), (2, 0): (0, 3), (3, 0): (0, 4),
            (0, 1): (0, 2), (1, 1): (1, 1), (2, 1): (0, 4), (3, 1): (0, 4)}

    def mask_of(t, d):
        n = SEEN[t, d][1]
        if d == 0:
            return MASK[:, 0, (4 - n) * P:HALF]
        if t == 3:
            return MASK[:, 2, :]
        return MASK[:, 1, {0: 2, 1: 2, 2: 0}[t] * P:({0: 2, 1: 2, 2: 0}[t] + n) * P]

    @phase
    def mlstm_attend():
        DAT, at = {}, 0
        for t in ALL:
            for d in range(2):
                DAT[t, d] = at
                at += SEEN[t, d][1] * P
        ITER = [(h, t) for h in range(MH) for t in ALL]
        N = len(ITER)
        DBUF = [2 * SLOT, W_AT[2], 0, WCH]
        dm = lambda h, t, d: region(DBUF[h] + DAT[t, d], SEEN[t, d][1] * P)
        big = {0: 1, 1: 0, 2: 1, 3: 1}
        M = [small[:, a:a + 8] for a in (96, 104)]
        nM = [small[:, a:a + 8] for a in (112, 120)]
        sm = [small[:, a:a + 8] for a in (128, 136)]
        gd = [small[:, a:a + 8] for a in (144, 152)]
        den = [small[:, a:a + 8] for a in (160, 168)]
        rr = [small[:, a:a + 8] for a in (176, 184)]
        ssq, std, rstd = small[:, 192:208], small[:, 208:224], small[:, 224:240]
        PT = [S1[:, b, 0:HALF] for b in range(2)]
        junk = [S1[:, b, HALF:HALF + 256] for b in range(2)]
        ab, aD, aM, ex, gu_, s_mm, td, pr, tr, pt, pv, ro, sq, fin, chain = (sem(f"matt_{n}") for n in (
            "rows", "masked", "negmax", "exp", "guard", "scores", "products", "weights", "turned", "copied",
            "heads", "gated", "squares", "final", "chain"))
        zero, filled = sem("matt_zero"), sem("matt_filled")
        with nc.Block() as block:
            @block.gpsimd
            def _(pool):
                pool.memset(G[:, 0, :], 0.0).then_inc(zero, 1)

            @block.sync
            def _(sp):
                sp.wait_ge(zero, 1)
                for dram in (xs, ys):
                    sp.dma_start(dram[0:TMAX * B, :].rearrange("(n p) d -> p n d", p=P),
                                 bc(G[:, 0:1, :], [P, TMAX * B // P, D])).then_inc(filled, 16)
                sp.dma_start(xs[TMAX * B:XROWS, :], G[0:B, 0, :]).then_inc(filled, 16)
                sp.wait_ge(filled, 48)

            @block.tensor
            def _(pe):
                def rows(h):
                    if h:
                        pe.wait_ge(aD, h)
                    for d in range(2):
                        for t in ALL:
                            last = pe.matmul(bank[d][:, t * P:(t + 1) * P], bc(ag[:, t, 4 * d + h:4 * d + h + 1], [P, P]),
                                             ident[:], start=True, stop=True)
                    last.then_inc(ab, 1)

                def scores(h, t):
                    i = 4 * h + t
                    n = 256 if t < 2 else 512
                    if i >= 2:
                        pe.wait_ge(td, i - 1)
                    for kk in range(2):
                        last = pe.matmul(bank[2 + i % 2][:, 0:n], qkT[:, 2 * h + kk, t * P:(t + 1) * P],
                                         qkT[:, 8 + 2 * h + kk, 0:n], start=(kk == 0), stop=(kk == 1))
                    last.then_inc(s_mm, 1)

                def turn(h, t):
                    i = 4 * h + t
                    pe.wait_ge(pr, i + 1)
                    if i >= 2:
                        pe.wait_ge(pt, i - 1)
                    n = SEEN[t, big[t]][1]
                    for s in range(n):
                        last = pe.transpose(bank[4 + i % 2][:, s * P:(s + 1) * P], dm(h, t, big[t])[:, s * P:(s + 1) * P], ident[:])
                    last.then_inc(tr, 1)

                def heads(h, t):
                    i = 4 * h + t
                    pe.wait_ge(pt, i + 1)
                    if i >= 2:
                        pe.wait_ge(ro, i - 1)
                        pe.wait_ge(sq, i - 1)
                    k0, n = SEEN[t, big[t]]
                    for s in range(n):
                        last = pe.matmul(bank[6 + i % 2][:, 0:MDH], PT[i % 2][:, s * P:(s + 1) * P],
                                         V[:, k0 + s, h * MDH:(h + 1) * MDH], start=(s == 0), stop=(s == n - 1))
                    last.then_inc(pv, 1)

                rows(0)
                rows(1)
                scores(0, 0)
                scores(0, 1)
                for i, (h, t) in enumerate(ITER):
                    if t == 0 and h + 2 < MH:
                        rows(h + 2)
                    if i + 2 < N:
                        scores(*ITER[i + 2])
                    turn(h, t)
                    if i:
                        heads(*ITER[i - 1])
                heads(*ITER[N - 1])

            @block.vector
            def _(dve):
                ch = Chain(chain)

                def masked(h, t):
                    dve.wait_ge(ab, h + 1)
                    for d in range(2):
                        k0, n = SEEN[t, d]
                        last = dve.tensor_tensor_reduce(dm(h, t, d), bank[d][:, k0 * P:(k0 + n) * P], mask_of(t, d),
                                                        1.0, 0.0, ALU.add, ALU.max, M[h % 2][:, 2 * t + d:2 * t + d + 1])
                    if t == 3:
                        last.then_inc(aD, 1)
                        dve.wait_ge(aD, h + 1)
                        dve.tensor_scalar(nM[h % 2], M[h % 2], -1.0, None, ALU.mult).then_inc(aM, 1)
                        fv = small[:, 32:64].rearrange("p (t d h) -> p t d h", t=TILES, d=2)[:, :, :, h]
                        dve.tensor_tensor(sm[h % 2].rearrange("p (t d) -> p t d", d=2), M[h % 2].rearrange("p (t d) -> p t d", d=2),
                                          fv, ALU.add).then_inc(aM, 1)

                def weights(h, t):
                    i = 4 * h + t
                    dve.wait_ge(s_mm, i + 1)
                    dve.wait_ge(ex, 2 * i + 2)
                    both = slice(2 * t, 2 * t + 2)
                    dd, r = den[h % 2][:, both], rr[h % 2][:, both]
                    for d in range(2):
                        k0, n = SEEN[t, d]
                        v = dm(h, t, d)
                        last = dve.tensor_tensor_reduce(v, bank[2 + i % 2][:, k0 * P:(k0 + n) * P], v, MDH ** -0.5, 0.0,
                                                        ALU.mult, ALU.add, dd[:, d:d + 1])
                    last.then_inc(td, 1)
                    dve.wait_ge(td, i + 1)
                    ch.link(dve, dve.scalar_tensor_tensor(out=dd, in0=dd, scalar=-1.0, in1=dd, op0=ALU.mult, op1=ALU.max))
                    dve.wait_ge(gu_, h + 1)
                    ch.link(dve, dve.tensor_tensor(dd, dd, gd[h % 2][:, both], ALU.max))
                    ch.link(dve, dve.reciprocal(r, dd))
                    b = big[t]
                    o = 1 - b
                    kb, ko, no = SEEN[t, b][0], SEEN[t, o][0], SEEN[t, o][1]
                    whole, part = dm(h, t, b), dm(h, t, o)
                    ch.link(dve, dve.tensor_scalar(whole, whole, r[:, b:b + 1], None, ALU.mult))
                    into = whole[:, (ko - kb) * P:(ko - kb + no) * P]
                    dve.scalar_tensor_tensor(out=into, in0=part, scalar=r[:, o:o + 1], in1=into,
                                             op0=ALU.mult, op1=ALU.add).then_inc(pr, 1)

                def gated(h, t):
                    i = 4 * h + t
                    dve.wait_ge(pv, i + 1)
                    o = O[:, t, h * MDH:(h + 1) * MDH]
                    dve.tensor_tensor(o, bank[6 + i % 2][:, 0:MDH], o, ALU.mult).then_inc(ro, 1)

                for h in range(2):
                    for t in ALL:
                        masked(h, t)
                for i, (h, t) in enumerate(ITER):
                    weights(h, t)
                    if h + 2 < MH:
                        masked(h + 2, t)
                    if i >= 2:
                        gated(*ITER[i - 2])
                gated(*ITER[N - 2])
                gated(*ITER[N - 1])
                dve.wait_ge(fin, 1)
                dve.reciprocal(rstd, std).then_inc(fin, 1)
                dve.wait_ge(fin, 2)
                dve.wait_ge(ro, 16)
                for h in (0, 1, 2):
                    for t in ALL:
                        o = O[:, t, h * MDH:(h + 1) * MDH]
                        dve.tensor_scalar(o, o, rstd[:, 4 * h + t:4 * h + t + 1], None, ALU.mult).then_inc(fin, 1)

            @block.scalar
            def _(act):
                def exps(h, t):
                    act.wait_ge(aM, 2 * h + 2)
                    for d in range(2):
                        v = dm(h, t, d)
                        act.activation(v, v, ACT.Exp, bias=nM[h % 2][:, 2 * t + d:2 * t + d + 1]).then_inc(ex, 1)
                    if t == 0:
                        act.activation(gd[h % 2], sm[h % 2], ACT.Exp, scale=-1.0).then_inc(gu_, 1)

                def square(i):
                    act.wait_ge(ro, i + 1)
                    act.activation(junk[i % 2], bank[6 + i % 2][:, 0:MDH], ACT.Square, accum_out=ssq[:, i:i + 1]).then_inc(sq, 1)

                for t in ALL:
                    exps(0, t)
                for i, (h, t) in enumerate(ITER):
                    act.wait_ge(tr, i + 1)
                    if i >= 2:
                        act.wait_ge(pv, i - 1)
                    n = SEEN[t, big[t]][1] * P
                    act.activation(PT[i % 2][:, 0:n], bank[4 + i % 2][:, 0:n], ACT.Copy).then_inc(pt, 1)
                    if h + 1 < MH:
                        exps(h + 1, t)
                    if i >= 2:
                        square(i - 2)
                square(N - 2)
                square(N - 1)
                act.wait_ge(sq, 16)
                act.activation(std, ssq, ACT.Sqrt, bias=eps[:], scale=1.0 / MDH).then_inc(fin, 1)
                act.wait_ge(fin, 2)
                for t in ALL:
                    o = O[:, t, 3 * MDH:4 * MDH]
                    act.activation(o, o, ACT.Copy, scale=rstd[:, 12 + t:13 + t]).then_inc(gu_, 1)

    def gate_rows(pe, act, layer, part, streams, mm, ev):
        if pe is not None:
            for si, s in enumerate(streams):
                for hf in range(2):
                    for k in range(4):
                        last = pe.matmul(bank[2 * si + hf][:, k * P:(k + 1) * P],
                                         bc(modT[:, layer, 8 * part + 4 * hf + k, s:s + 1], [P, P]), ident[:], start=True, stop=True)
                    last.then_inc(mm, 1)
        if act is not None:
            for si, s in enumerate(streams):
                for hf in range(2):
                    act.wait_ge(mm, 2 * si + hf + 1)
                    act.activation(G[:, s, hf * HALF:(hf + 1) * HALF], bank[2 * si + hf][:], ACT.Copy).then_inc(ev, 1)

    @phase
    def output(layer, tiles, src, colv, wkey, prefetch):
        nt = len(tiles)
        streams = [0, 1] if nt == 4 else [1]
        gm, ge, tr, ev, ym, yt, ya, cl = (sem(f"out{layer}_{n}") for n in (
            "gate_mm", "gate", "turned", "columns", "product", "gated", "added", "col"))
        squares, std = sem(f"out{layer}_squares"), sem(f"out{layer}_std")
        rT = region(W_AT[2] if layer else 2 * SLOT, KT, nt * P)
        tmp = [S1[:, b, 0:HALF] for b in range(2)]
        with nc.Block() as block:
            @block.sync
            def _(sp):
                load_rw(sp, layer)
                prefetch(sp)

            @block.tensor
            def _(pe):
                gate_rows(pe, None, layer, 2, streams, gm, ge)
                for k in range(KT):
                    if k == 4:
                        pe.wait_ge(ge, 2 * len(streams))
                    for j in range(nt):
                        last = pe.transpose(bank[(4 + k) % 8][:, j * P:(j + 1) * P], src[:, j, k * P:(k + 1) * P], ident[:])
                    last.then_inc(tr, 1)
                pe.wait_ge(ev, KT)
                w = [chunk(pe, AT[(wkey, 0)]), chunk(pe, AT[(wkey, 1)])]
                for j in range(nt):
                    for cc in range(2):
                        for k in range(KT):
                            last = pe.matmul(bank[(2 * j + cc) % 8][:], rT[:, k, j * P:(j + 1) * P], w[cc][:, k, :],
                                             start=(k == 0), stop=(k == KT - 1))
                        last.then_inc(ym, 1)

            @block.scalar
            def _(act):
                gate_rows(None, act, layer, 2, streams, gm, ge)
                if layer:
                    act.wait_ge(cl, 1)
                for k in range(1, KT, 2):
                    act.wait_ge(tr, k + 1)
                    act.activation(rT[:, k, :], bank[(4 + k) % 8][:, 0:nt * P], ACT.Copy, scale=colv(k)).then_inc(ev, 1)
                for j, t in enumerate(tiles):
                    act.wait_ge(ya, 2 * j + 2)
                    row_squares(act, j, t, MASK_ROW, squares)
                row_roots(act, nt, squares, std)

            @block.vector
            def _(dve):
                if layer:
                    dve.tensor_scalar(small[:, 28:29], vT[:, 2, SUBG:SUBG + 1], 1.0 - LAMBDA_INIT, None, ALU.mult).then_inc(cl, 1)
                    dve.wait_ge(cl, 1)
                for k in range(0, KT, 2):
                    dve.wait_ge(tr, k + 1)
                    dve.tensor_scalar(rT[:, k, :], bank[(4 + k) % 8][:, 0:nt * P], colv(k), None, ALU.mult).then_inc(ev, 1)
                dve.wait_ge(ge, 2 * len(streams))
                for j, t in enumerate(tiles):
                    for cc in range(2):
                        u = 2 * j + cc
                        dve.wait_ge(ym, u + 1)
                        if u >= 2:
                            dve.wait_ge(ya, u - 1)
                        dve.tensor_tensor(tmp[u % 2], bank[u % 8][:], G[:, t // 2, cc * HALF:(cc + 1) * HALF], ALU.mult).then_inc(yt, 1)
                        dve.wait_ge(yt, u + 1)
                        xx = X[:, t, cc * HALF:(cc + 1) * HALF]
                        dve.tensor_tensor(xx, xx, tmp[u % 2], ALU.add).then_inc(ya, 1)
                row_inverses(dve, nt, std)

    @phase
    def route(layer, tiles, prefetch):
        nt = len(tiles)
        mask = MASK[:].rearrange("p a b -> p (a b)")
        state = {"at": 0}

        def take(*shape):
            n = math.prod(shape)
            v = mask[:, state["at"]:state["at"] + n]
            state["at"] += n
            return v.rearrange("p (t n) -> p t n", t=shape[0]) if len(shape) == 2 else v

        lg, el, eq, oh1, oh2, cnt, rk, tmp = (take(nt, 36), *(take(nt, NE) for _ in range(7)))
        gx, gq = take(nt, NG), take(nt, NG)
        m1, m2, mg, gs, e2, r, t1, t2 = (take(nt) for _ in range(8))
        tot = take(nt, NE)
        ncol, nb, base = take(1), take(1), take(NE)
        key32 = iof[:, 0:NE]
        lgt, lgc = sem(f"route{layer}_logit_rows"), sem(f"route{layer}_logit_rows_copied")
        lgm, dv, ac, cn, pm, hb, nbd, tbm, tbd, pd, rt, re, chain = (sem(f"route{layer}_{n}") for n in (
            "logits", "vector", "scalar", "counts", "prefix", "rows_free", "blocks", "table_mm", "table", "pos",
            "row_turned", "row_ready", "chain"))
        sca = sem(f"route{layer}_scattered")
        rows = [S1[:, 0, :], S1[:, 1, :], G[:, 0, :], G[:, 1, :]]
        with nc.Block() as block:
            @block.sync
            def _(sp):
                prefetch(sp)

            @block.tensor
            def _(pe):
                pe.wait_ge(rw_loaded, 32 * (layer + 1))
                n, t0 = nt * P, tiles[0] * P
                for k in range(0, KT, 2):
                    for q in range(4):
                        kk, hf = k + q // 2, q % 2
                        last = pe.matmul(bank[3][32 * q:32 * q + 32, 0:n], rw[:, kk, 32 * hf:32 * hf + 32], h2T[:, kk, t0:t0 + n],
                                         start=(k == 0), stop=(k == KT - 2), skip_group_check=True)
                last.then_inc(lgt, 1)
                pe.wait_ge(lgc, 1)
                for j in range(nt):
                    last = pe.transpose(bank[0][:, j * P:(j + 1) * P], S2[:, 0, j * P:(j + 1) * P], ident[:])
                last.then_inc(lgm, 1)
                for j, t in enumerate(tiles):
                    for hf in range(2):
                        u = 2 * j + hf
                        if u >= 4:
                            pe.wait_ge(re, u - 3)
                        for k in range(4):
                            last = pe.transpose(bank[4 + u % 4][:, k * P:(k + 1) * P], h2T[:, 4 * hf + k, t * P:(t + 1) * P], ident[:])
                        last.then_inc(rt, 1)
                pe.wait_ge(cn, 1)
                flat = cnt.rearrange("p t n -> p (t n)")
                pe.matmul(bank[1][:, 0:nt * NE], before[:], flat, start=True, stop=True)
                pe.matmul(bank[1][:, 128:128 + nt * NE], ones[:], flat, start=True, stop=True)
                for j in range(nt):
                    last = pe.matmul(bank[2][0:NE, 0:P], cnt[:, j, :], ones[:], start=(j == 0), stop=(j == nt - 1))
                last.then_inc(pm, 1)
                pe.wait_ge(nbd, 2)
                pe.matmul(bank[3][:, 0:NE], bc(nb[0:NE, :], [NE, P]), ident[0:NE, 0:NE], start=True, stop=True)
                pe.matmul(bank[3][:, NE:2 * NE], bc(nb[0:NE, :], [NE, P]), before[0:NE, 0:NE], start=True, stop=True)
                pe.matmul(bank[3][:, 2 * NE:2 * NE + 1], bc(nb[0:NE, :], [NE, P]), ones[0:NE, 0:1], start=True, stop=True).then_inc(tbm, 1)

            @block.scalar
            def _(act):
                act.wait_ge(dv, 1)
                act.activation(gx, gx, ACT.Exp).then_inc(ac, 1)
                for u in range(2 * nt):
                    act.wait_ge(rt, u + 1)
                    if u == 4:
                        act.wait_ge(lgm, 1)
                    act.activation(rows[u // 2][:, (u % 2) * HALF:(u % 2 + 1) * HALF], bank[4 + u % 4][:], ACT.Copy).then_inc(re, 1)
                    if u == 3:
                        act.wait_ge(dv, 2)
                        act.activation(e2, e2, ACT.Exp).then_inc(ac, 1)

            @block.vector
            def _(dve):
                ch = Chain(chain)
                L = lambda ins: ch.link(dve, ins)
                w3 = lambda v, n: bc(v.unsqueeze(2), [P, nt, n])
                dve.wait_ge(lgt, 1)
                dve.tensor_copy(S2[:, 0, 0:nt * P], bank[3][:, 0:nt * P]).then_inc(lgc, 1)
                dve.wait_ge(lgm, 1)
                both = bank[0][:, 0:nt * P].rearrange("p (t a n) -> p t a n", t=nt, a=2)
                L(dve.tensor_copy(lg, both[:, :, 0, 0:36]))
                L(dve.tensor_tensor(lg, lg, both[:, :, 1, 0:36], ALU.add))
                L(dve.tensor_tensor(lg, lg,
                                    bc(rowb[:, GRP + 36 * layer:GRP + 36 * layer + 36].unsqueeze(1), [P, nt, 36]), ALU.add))
                L(dve.tensor_reduce(mg, lg[:, :, 0:NG], AX_X, ALU.max))
                dve.tensor_tensor(gx, lg[:, :, 0:NG], w3(mg, NG), ALU.subtract).then_inc(dv, 1)
                L(dve.tensor_tensor(gq, lg[:, :, 0:NG], w3(mg, NG), ALU.is_equal))
                L(dve.tensor_tensor(gq, gq, bc(iof[:, NE - NG:NE].unsqueeze(1), [P, nt, NG]), ALU.mult))
                L(dve.tensor_reduce(t1, gq, AX_X, ALU.max))
                L(dve.tensor_tensor(gq, gq, w3(t1, NG), ALU.is_equal))
                L(dve.tensor_scalar(gq, gq, -NEG, NEG, ALU.mult, ALU.add))
                for g in range(NG):
                    L(dve.tensor_tensor(el[:, :, NPG * g:NPG * g + NPG], lg[:, :, NG + NPG * g:NG + NPG * g + NPG],
                                        w3(gq[:, :, g], NPG), ALU.add))

                def top(m, oh):
                    L(dve.tensor_reduce(m, el, AX_X, ALU.max))
                    L(dve.tensor_tensor(eq, el, w3(m, NE), ALU.is_equal))
                    L(dve.tensor_tensor(eq, eq, bc(key32.unsqueeze(1), [P, nt, NE]), ALU.mult))
                    L(dve.tensor_reduce(t1, eq, AX_X, ALU.max))
                    L(dve.tensor_tensor(oh, eq, w3(t1, NE), ALU.is_equal))

                top(m1, oh1)
                L(dve.scalar_tensor_tensor(out=el, in0=oh1, scalar=4 * NEG, in1=el, op0=ALU.mult, op1=ALU.add))
                top(m2, oh2)
                dve.tensor_tensor(e2, m2, m1, ALU.subtract).then_inc(dv, 1)
                dve.tensor_tensor(cnt, oh1, oh2, ALU.add).then_inc(cn, 1)
                dve.wait_ge(ac, 1)
                L(dve.tensor_reduce(gs, gx, AX_X, ALU.add))
                dve.wait_ge(ac, 2)
                L(dve.tensor_scalar(r, e2, 1.0, None, ALU.add))
                L(dve.tensor_tensor(r, r, gs, ALU.mult))
                L(dve.reciprocal(gat[:, 0, 0:nt], r))
                L(dve.tensor_tensor(gat[:, 1, 0:nt], gat[:, 0, 0:nt], e2, ALU.mult))
                dve.wait_ge(pm, 1)
                dve.tensor_copy(ncol[0:NE, :], bank[2][0:NE, 0:1]).then_inc(nbd, 1)
                dve.wait_ge(nbd, 1)
                dve.tensor_scalar(tmp[0:NE, 0, 0:NBMAX - 1], iof[0:NE, NE:NE + NBMAX - 1], ncol[0:NE, :], 1.0,
                                  ALU.is_lt, ALU.add, accum_out=nb[0:NE, :]).then_inc(nbd, 1)
                L(dve.tensor_copy(rk.rearrange("p t n -> p (t n)"), bank[1][:, 0:nt * NE]))
                L(dve.tensor_copy(tot.rearrange("p t n -> p (t n)"), bank[1][:, 128:128 + nt * NE]))
                for j in range(1, nt):
                    L(dve.tensor_tensor(rk[:, j, :], rk[:, j, :], tot[:, j - 1, :], ALU.add))
                    if j + 1 < nt:
                        L(dve.tensor_tensor(tot[:, j, :], tot[:, j, :], tot[:, j - 1, :], ALU.add))
                dve.wait_ge(tbm, 1)
                dve.tensor_copy(tab[0:1, :], bank[3][0:1, 0:2 * NE + 1]).then_inc(tbd, 1)
                L(dve.tensor_scalar(base, bank[3][:, NE:2 * NE], float(B), None, ALU.mult))
                L(dve.tensor_tensor(rk, rk, bc(base.unsqueeze(1), [P, nt, NE]), ALU.add))
                for o, oh in enumerate((oh1, oh2)):
                    L(dve.tensor_tensor(tmp, rk, oh, ALU.mult))
                    L(dve.tensor_reduce(t2, tmp, AX_X, ALU.add))
                    dve.tensor_copy(pos[:, o, 0:nt], t2).then_inc(pd, 1)
                    dve.wait_ge(pd, o + 1)

            @block.gpsimd
            def _(pool):
                pool.wait_ge(pd, 2)
                for j in range(nt):
                    pool.wait_ge(re, 2 * j + 2)
                    for o in range(2):
                        pool.indirect_dma_start(
                            out=xs, out_offset=bass.IndirectOffsetOnAxis(ap=pos[:, o, j:j + 1].bitcast(U32), axis=0),
                            in_=rows[j], in_offset=None).then_inc(sca, 16)
                pool.wait_ge(sca, 32 * nt)

    N_OF = [len(range(s, NE, 3)) for s in range(3)]

    GATE_UP, DOWN = range(4), range(4, 6)

    def load_expert(eng, layer, e, s, i, pieces=range(6), down_is_free=lambda: None):
        gsrc = e_w_gu[layer].rearrange("e (k p) n -> p e k n", p=P)
        dsrc = e_w_dn[layer].rearrange("e (k p) n -> p e k n", p=P)
        for piece in pieces:
            ks = slice(2 * (piece % 4), 2 * (piece % 4) + 2)
            if piece >= 2:
                eng.wait_ge(gu_loaded[s][piece % 2], 32 * i + (16 if piece < 4 else 32))
            if piece == 4:
                down_is_free()
            if piece < 4:
                eng.dma_start(gu_w[s][:, ks, :].unsqueeze(1), gsrc[:, bass.ds(e, 1), ks, :]).then_inc(gu_loaded[s][piece % 2], 16)
            else:
                eng.dma_start(dn_w[s][:, ks, :].unsqueeze(1), dsrc[:, bass.ds(e, 1), ks, :]).then_inc(dn_loaded[s][piece % 2], 16)

    @phase
    def experts(layer):
        a0 = W_AT[2]
        xr = region(a0, 256)
        xT = region(a0 + 256, 256)
        sg, av, aT = (region(a0 + 512 + i * P, P) for i in range(3))
        yb = region(a0 + 1024, 256)
        xl, xt_t, xt_c, gu_mm, si_, a_, at_t, at_c, dn_mm, yc, yst = (sem(f"moe{layer}_{n}") for n in (
            "rows", "rows_turned", "columns", "gate_up", "silu", "hidden", "hidden_turned", "hidden_columns",
            "down", "copied", "stored"))
        quarters = lambda dram, t: dram[bass.ds(t * B, B), :].rearrange("t (c n) -> c t n", c=4)
        before_layer = [layer * n for n in N_OF]

        def blocks_of(eng, e):
            return (eng.value_load(tab[0:1, bass.ds(e, 1)], min_val=1, max_val=NBMAX),
                    eng.value_load(tab[0:1, bass.ds(e + NE, 1)], min_val=0, max_val=TMAX - 1))

        def total(eng):
            return eng.value_load(tab[0:1, 2 * NE:2 * NE + 1], min_val=NE, max_val=TMAX)

        with nc.Block() as block:
            @block.sync
            def _(sp):
                def refill(e, s, i):
                    nb, t0 = blocks_of(sp, e - 3)
                    sp.wait_ge(gu_mm, t0 + nb)
                    load_expert(sp, layer, e, s, i + before_layer[s],
                                down_is_free=lambda: sp.wait_ge(dn_mm, t0 + nb))

                with sp.Fori(1, NE // 3) as i:
                    for s in range(3):
                        refill(i * 3 + s, s, i)
                for s in range(NE % 3):
                    refill(NE // 3 * 3 + s, s, NE // 3)

            @block.gpsimd
            def _(pool):
                def load(t):
                    pool.dma_start(xr, quarters(xs, t)).then_inc(xl, 16)

                n = total(pool)
                load(0)
                with pool.Fori(1, n + 1) as t:
                    pool.wait_ge(xt_t, t)
                    load(t)
                pool.wait_ge(xl, (n + 1) * 16)

            @block.tensor
            def _(pe):
                def turn_rows(t):
                    pe.wait_ge(xl, (t + 1) * 16)
                    for hf in range(2):
                        last = pe.transpose(bank[0][:, hf * P:(hf + 1) * P], xr[:, hf * P:(hf + 1) * P], ident[:])
                    last.then_inc(xt_t, 1)

                def one_block(t, s, i):
                    pe.wait_ge(xt_c, t + 1)
                    for b in range(2):
                        pe.wait_ge(gu_loaded[s][b], (i + 1) * 32)
                    for k in range(KT):
                        w = gu_w[s][:, k, :].rearrange("p (h n) -> p h n", h=2)
                        lhs = xT[:, (k % 2) * P + (k // 2) * B:(k % 2) * P + (k // 2) * B + B]
                        for q in range(4):
                            last = pe.matmul(bank[1][32 * q:32 * q + 32, 0:256], lhs, w[:, :, q * P:(q + 1) * P],
                                             start=(k == 0), stop=(k == KT - 1), skip_group_check=True)
                    last.then_inc(gu_mm, 1)
                    turn_rows(t + 1)
                    pe.wait_ge(a_, t + 1)
                    pe.transpose(bank[2][:, 0:P], av, ident[:]).then_inc(at_t, 1)
                    pe.wait_ge(at_c, t + 1)
                    for b in range(2):
                        pe.wait_ge(dn_loaded[s][b], (i + 1) * 16)
                    pe.wait_ge(yc, t + 1)
                    for f in range(DE // P):
                        for q in range(4):
                            last = pe.matmul(bank[3][32 * q:32 * q + 32, 0:256], aT[:, f * B:(f + 1) * B],
                                             dn_w[s][:, f, q * 256:(q + 1) * 256], start=(f == 0), stop=(f == DE // P - 1),
                                             skip_group_check=True)
                    last.then_inc(dn_mm, 1)

                def expert(e, s, i):
                    nb, t0 = blocks_of(pe, e)
                    with pe.Fori(0, nb) as j:
                        one_block(t0 + j, s, i + before_layer[s])

                turn_rows(0)
                with pe.Fori(0, NE // 3) as i:
                    for s in range(3):
                        expert(i * 3 + s, s, i)
                for s in range(NE % 3):
                    expert(NE // 3 * 3 + s, s, NE // 3)

            @block.vector
            def _(dve):
                def columns(t):
                    dve.wait_ge(xt_t, t + 1)
                    dve.tensor_copy(xT, bank[0][:, 0:256]).then_inc(xt_c, 1)

                n = total(dve)
                columns(0)
                with dve.Fori(0, n) as t:
                    dve.wait_ge(si_, t + 1)
                    dve.tensor_tensor(av, sg, bank[1][:, P:2 * P], ALU.mult).then_inc(a_, 1)
                    columns(t + 1)
                    dve.wait_ge(at_t, t + 1)
                    dve.tensor_copy(aT, bank[2][:, 0:P]).then_inc(at_c, 1)

            @block.scalar
            def _(act):
                act.activation(yb[:, 0:1], eps[:], ACT.Copy).then_inc(yc, 1)
                act.dma_start(tabd[layer:layer + 1, :], tab[0:1, :]).then_inc(yst, 16)
                n = total(act)
                with act.Fori(0, n) as t:
                    act.wait_ge(gu_mm, t + 1)
                    act.activation(sg, bank[1][:, 0:P], ACT.Silu).then_inc(si_, 1)
                    act.wait_ge(dn_mm, t + 1)
                    act.wait_ge(yst, (t + 1) * 16)
                    act.activation(yb, bank[3][:, 0:256], ACT.Copy).then_inc(yc, 1)
                    act.wait_ge(yc, t + 2)
                    act.dma_start(quarters(ys, t), yb).then_inc(yst, 16)
                act.wait_ge(yst, (n + 1) * 16)
                act.activation(sg[:, 0:1], eps[:], ACT.Copy).then_inc(yc, 1)

    @phase
    def combine(layer, tiles, extra_sync=None):
        nt = len(tiles)
        streams = [0, 1] if nt == 4 else [1]
        Y = region(SLOT, 2 * nt, D)
        gm, ge, chain, xo, st = (sem(f"comb{layer}_{n}") for n in ("gate_mm", "gate", "chain", "added", "stored"))
        yl = [sem(f"comb{layer}_rows{j}") for j in range(nt)]
        squares, std = sem(f"comb{layer}_squares"), sem(f"comb{layer}_std")
        with nc.Block() as block:
            @block.gpsimd
            def _(pool):
                for j in range(nt):
                    for o in range(2):
                        pool.indirect_dma_start(
                            out=Y[:, 2 * j + o, :], out_offset=None, in_=ys[0:TMAX * B, :],
                            in_offset=bass.IndirectOffsetOnAxis(ap=pos[:, o, j:j + 1].bitcast(U32), axis=0)).then_inc(yl[j], 16)

            @block.tensor
            def _(pe):
                gate_rows(pe, None, layer, 5, streams, gm, ge)

            @block.scalar
            def _(act):
                gate_rows(None, act, layer, 5, streams, gm, ge)
                if not layer:
                    for j, t in enumerate(tiles):
                        act.wait_ge(xo, j + 1)
                        row_squares(act, j, t, S1[:, 0, :], squares)
                    row_roots(act, nt, squares, std)

            @block.vector
            def _(dve):
                ch = Chain(chain)
                dve.wait_ge(ge, 2 * len(streams))
                for j, t in enumerate(tiles):
                    dve.wait_ge(yl[j], 32)
                    a, b = Y[:, 2 * j, :], Y[:, 2 * j + 1, :]
                    ch.link(dve, dve.tensor_scalar(a, a, gat[:, 0, j:j + 1], None, ALU.mult))
                    ch.link(dve, dve.scalar_tensor_tensor(out=a, in0=b, scalar=gat[:, 1, j:j + 1], in1=a, op0=ALU.mult, op1=ALU.add))
                    ch.link(dve, dve.tensor_tensor(a, a, G[:, t // 2, :], ALU.mult))
                    dve.tensor_tensor(X[:, t, :], X[:, t, :], a, ALU.add).then_inc(xo, 1)
                if not layer:
                    row_inverses(dve, nt, std)

            @block.sync
            def _(sp):
                if extra_sync:
                    for j in range(nt):
                        sp.wait_ge(yl[j], 32)
                    extra_sync(sp)
                if layer:
                    for j, t in enumerate(tiles):
                        sp.wait_ge(xo, j + 1)
                        sp.dma_start(out[0, (t - 2) * P:(t - 1) * P, :], X[:, t, :]).then_inc(st, 16)
                    sp.wait_ge(st, 16 * nt)

    kT = region(SLOT, DH, TOK)
    V1 = region(SLOT + 4096, TILES, D)
    qT = region(SLOT + GU, DH, NLAT)
    A1 = region(SLOT + GU + 2048, 2, D)

    @phase
    def diff_project():
        tabs = MASK[:].rearrange("p a b -> p (a b)")
        cs = S2[:, 0, 0:256].rearrange("p (t w n) -> p t w n", t=TILES, w=2)
        Ck, Sk, Cq, Sq = (tabs[:, a:a + n * DDH].rearrange("p (t a h f) -> p t a h f", t=n, a=2, h=2)
                          for a, n in ((0, 4), (256, 4), (512, 2), (640, 2)))
        ssd, std, rstd = small[:, 96:104], small[:, 104:112], small[:, 112:120]
        sqb, xnb, t1b, t2b = S1[:, 0, 0:HALF], S1[:, 0, HALF:D], S1[:, 1, 0:HALF], S1[:, 1, HALF:D]
        kqb = [S2[:, 0, 256:256 + HALF], S2[:, 1, 0:HALF]]
        unit, ev, rp, sqs, st, xo, tr, te, chain = (sem(f"dproj_{n}") for n in (
            "unit", "evacuated", "rope", "squares", "std", "rows", "turned", "columns", "chain"))
        units = []
        for cidx in (2, 3, 0, 1, 4, 5):
            kind = "qkv"[cidx // 2]
            for t in (LAT if kind == "q" else ALL):
                units.append((cidx, kind, cidx % 2, t))
        nqk = sum(u[1] != "v" for u in units)
        plan = []
        n_at = 0
        for cidx in (2, 3, 0, 1, 4, 5):
            mine = [n for n, u in enumerate(units) if u[0] == cidx]
            n = AT[("d_in", cidx)]
            ada = [m for m in (n + 1, n + 2) if STREAM[m][0] == "ada"]
            plan.append(("unit", mine[0]))
            rest = mine[1:]
            for m in ada:
                plan.append(("mul", m))
                if rest:
                    plan.append(("unit", rest.pop(0)))
                plan.append(("turn", m))
            plan += [("unit", r) for r in rest]
        multiplied.update({AT[("d_in", u[0])]: (unit, n + 1) for n, u in enumerate(units)})

        with nc.Block() as block:
            @block.sync
            def _(sp):
                sp.dma_start(cs, rope).then_inc(rp, 16)
                for n in range(AT[("d_in", 2)] + NW, AT[("d_out", 1)] + 1):
                    load_chunk(sp, n)

            @block.tensor
            def _(pe):
                def turn(n):
                    pe.wait_ge(xo, n + 1)
                    if n:
                        pe.wait_ge(te, n)
                    for q in range(4):
                        last = pe.transpose(bank[5][:, q * P:(q + 1) * P], kqb[n % 2][:, q * P:(q + 1) * P], ident[:])
                    last.then_inc(tr, 1)

                turned = 0
                for what, n in plan:
                    if what == "unit":
                        cidx, kind, hf, t = units[n]
                        w = chunk(pe, AT[("d_in", cidx)])
                        if n >= 4:
                            pe.wait_ge(ev, n - 3)
                        for k in range(KT):
                            last = pe.matmul(bank[n % 4][:], hT[:, k, t * P:(t + 1) * P], w[:, k, :], start=(k == 0), stop=(k == KT - 1))
                        last.then_inc(unit, 1)
                        while turned < min(n - 1, nqk):
                            turn(turned)
                            turned += 1
                    elif what == "mul":
                        ada_multiply(pe, n)
                    else:
                        ada_turn(pe, n)

            @block.scalar
            def _(act):
                def columns(n):
                    cidx, kind, hf, t = units[n]
                    act.wait_ge(tr, n + 1)
                    src = bank[5][:].rearrange("p (h n) -> p h n", h=4)
                    dst = kT[:, 4 * hf:4 * hf + 4, t * P:(t + 1) * P] if kind == "k" else qT[:, 4 * hf:4 * hf + 4, (t - 2) * P:(t - 1) * P]
                    act.activation(dst, src, ACT.Copy).then_inc(te, 1)

                for n, (cidx, kind, hf, t) in enumerate(units):
                    act.wait_ge(unit, n + 1)
                    if kind == "v":
                        act.activation(V1[:, t, hf * HALF:(hf + 1) * HALF], bank[n % 4][:], ACT.Copy).then_inc(ev, 1)
                        if n - 2 < nqk:
                            columns(n - 2)
                    else:
                        if n:
                            act.wait_ge(sqs, 2 * n)
                        act.activation(sqb, bank[n % 4][:], ACT.Square).then_inc(sqs, 1)
                        act.wait_ge(st, 2 * n + 1)
                        act.activation(std, ssd, ACT.Sqrt, bias=eps[:], scale=1.0 / DDH).then_inc(st, 1)
                        if n >= 2:
                            columns(n - 2)

            @block.vector
            def _(dve):
                ch = Chain(chain)
                L = lambda ins: ch.link(dve, ins)
                dve.wait_ge(rp, 16)
                for Ct, St, gcol, tiles in ((Ck, Sk, KG, ALL), (Cq, Sq, QG, LAT)):
                    gv = rowb[:, gcol:gcol + DDH].rearrange("p (a h f) -> p a h f", a=2, h=2)
                    for i, t in enumerate(tiles):
                        co = cs[:, t, 0, :].rearrange("p (a f) -> p a f", a=2)
                        so = cs[:, t, 1, :].rearrange("p (a f) -> p a f", a=2)
                        for h in range(2):
                            L(dve.tensor_tensor(Ct[:, i, :, h, :], gv[:, :, h, :], co, ALU.mult))
                            L(dve.scalar_tensor_tensor(out=St[:, i, :, h, :], in0=gv[:, :, 1 - h, :], scalar=(-1.0 if h == 0 else 1.0),
                                                       in1=so, op0=ALU.mult, op1=ALU.mult))

                def rows(n):
                    cidx, kind, hf, t = units[n]
                    Ct, St = (Ck[:, t], Sk[:, t]) if kind == "k" else (Cq[:, t - 2], Sq[:, t - 2])
                    dve.wait_ge(sqs, 2 * n + 1)
                    if n:
                        dve.wait_ge(st, 2 * n)
                    dve.tensor_reduce(ssd, sqb.rearrange("p (g n) -> p g n", g=8), AX_X, ALU.add).then_inc(st, 1)
                    dve.sem_inc(sqs, 1) if False else None
                    dve.wait_ge(st, 2 * n + 2)
                    dve.reciprocal(rstd, std).then_inc(sqs, 1)
                    dve.wait_ge(sqs, 2 * n + 2)
                    g8 = lambda v: v.rearrange("p (g n) -> p g n", g=8)
                    dve.tensor_tensor(g8(xnb), g8(bank[n % 4][:]), bc(rstd.unsqueeze(2), [P, 8, DDH]), ALU.mult).then_inc(ev, 1)
                    dve.wait_ge(ev, n + 1)
                    L(dve.tensor_tensor(g8(t1b), g8(xnb), bc(Ct.rearrange("p a h f -> p (a h f)").unsqueeze(1), [P, 8, DDH]), ALU.mult))
                    v = lambda b, h: b.rearrange("p (g a h f) -> p g a h f", g=8, a=2, h=2)[:, :, :, h, :]
                    for h in range(2):
                        L(dve.tensor_tensor(v(t2b, h), v(xnb, 1 - h), bc(St[:, :, h, :].unsqueeze(1), [P, 8, 2, 16]), ALU.mult))
                    if n >= 2:
                        dve.wait_ge(tr, n - 1)
                    dve.tensor_tensor(kqb[n % 2], t1b, t2b, ALU.add).then_inc(xo, 1)

                for what, n in plan:
                    if what == "unit":
                        if n < nqk:
                            rows(n)
                    elif what == "mul":
                        ada_copy(dve, n)
                    else:
                        ada_finish(dve, n)

    @phase
    def diff_attend():
        lamb = small[:, 96:104]
        E = [S1[:, b, :].rearrange("p (m n) -> p m n", m=2) for b in range(2)]
        PT = [S2[:, b, 0:HALF] for b in range(2)]
        stat = small[:, 128:256].rearrange("p (i n) -> p i n", i=16)
        ss, std, rstd = small[:, 256:272], small[:, 272:288], small[:, 288:304]
        s_mm, mx, ex, pr, tr, pt, pv, oc, fin, chain, lam_s, lam_a = (sem(f"datt_{n}") for n in (
            "scores", "max", "exp", "weights", "turned", "copied", "heads", "out", "final", "chain", "lam", "lam_exp"))
        ITER = [(j, h) for j in range(2) for h in range(DH)]
        scale = DDH ** -0.5
        with nc.Block() as block:
            @block.sync
            def _(sp):
                load_expert(sp, 1, 0, 0, N_OF[0])
                load_expert(sp, 1, 2, 2, N_OF[2], range(2))

            @block.tensor
            def _(pe):
                def scores(i):
                    j, h = ITER[i]
                    if i >= 2:
                        pe.wait_ge(ex, 2 * (i - 1))
                    for m in range(2):
                        lo = DDH * m
                        last = pe.matmul(bank[2 * (i % 2) + m][:], qT[lo:lo + DDH, h, j * P:(j + 1) * P], kT[lo:lo + DDH, h, :],
                                         start=True, stop=True)
                    last.then_inc(s_mm, 1)

                def turn(i):
                    pe.wait_ge(pr, i + 1)
                    if i >= 2:
                        pe.wait_ge(pt, i - 1)
                    for s in range(4):
                        last = pe.transpose(bank[4 + i % 2][:, s * P:(s + 1) * P], E[i % 2][:, 1, s * P:(s + 1) * P], ident[:])
                    last.then_inc(tr, 1)

                def heads(i):
                    j, h = ITER[i]
                    pe.wait_ge(pt, i + 1)
                    if i >= 2:
                        pe.wait_ge(oc, i - 1)
                    for s in range(4):
                        last = pe.matmul(bank[6 + i % 2][:, 0:DDV], PT[i % 2][:, s * P:(s + 1) * P], V1[:, s, h * DDV:(h + 1) * DDV],
                                         start=(s == 0), stop=(s == 3))
                    last.then_inc(pv, 1)

                scores(0)
                scores(1)
                for i in range(16):
                    if i + 2 < 16:
                        scores(i + 2)
                    turn(i)
                    if i:
                        heads(i - 1)
                heads(15)

            @block.scalar
            def _(act):
                act.wait_ge(lam_s, 2)
                act.activation(lamb[:, 2:4], lamb[:, 0:2], ACT.Exp).then_inc(lam_a, 1)

                def exps(i):
                    act.wait_ge(mx, 2 * i + 2)
                    if i >= 2:
                        act.wait_ge(tr, i - 1)
                    for m in range(2):
                        act.activation(E[i % 2][:, m, :], bank[2 * (i % 2) + m][:], ACT.Exp, bias=stat[:, i, m:m + 1], scale=scale,
                                       accum_out=stat[:, i, 2 + m:3 + m]).then_inc(ex, 1)

                exps(0)
                for i in range(16):
                    if i + 1 < 16:
                        exps(i + 1)
                    act.wait_ge(tr, i + 1)
                    if i >= 2:
                        act.wait_ge(pv, i - 1)
                    act.activation(PT[i % 2], bank[4 + i % 2][:], ACT.Copy).then_inc(pt, 1)
                act.wait_ge(fin, 1)
                act.activation(std, ss, ACT.Sqrt, bias=eps[:], scale=1.0 / DDV).then_inc(fin, 1)

            @block.vector
            def _(dve):
                ch = Chain(chain)
                L = lambda ins: ch.link(dve, ins)
                for o in range(2):
                    a = LQ + 2 * DDH * o
                    dve.tensor_tensor_reduce(small[:, 320:384], rowb[:, a:a + DDH], rowb[:, a + DDH:a + 2 * DDH], 1.0, 0.0,
                                             ALU.mult, ALU.add, lamb[:, o:o + 1]).then_inc(lam_s, 1)
                    dve.wait_ge(lam_s, o + 1)

                def maxima(i):
                    dve.wait_ge(s_mm, i + 1)
                    for m in range(2):
                        L(dve.tensor_reduce(stat[:, i, 4 + m:5 + m], bank[2 * (i % 2) + m][:], AX_X, ALU.max))
                    dve.tensor_scalar(stat[:, i, 0:2], stat[:, i, 4:6], -scale, None, ALU.mult).then_inc(mx, 2)

                maxima(0)
                maxima(1)
                dve.wait_ge(lam_a, 1)
                L(dve.tensor_tensor(lamb[:, 4:5], lamb[:, 3:4], lamb[:, 2:3], ALU.subtract))
                L(dve.tensor_scalar(lamb[:, 5:6], lamb[:, 4:5], LAMBDA_INIT, None, ALU.subtract))

                def head_out(i):
                    j, h = ITER[i]
                    dve.wait_ge(pv, i + 1)
                    dve.tensor_copy(A1[:, j, h * DDV:(h + 1) * DDV], bank[6 + i % 2][:, 0:DDV]).then_inc(oc, 1)

                def squares(j):
                    dve.wait_ge(oc, 8 * j + 8)
                    tmp = region(W_AT[2], D)
                    L(dve.tensor_tensor(tmp, A1[:, j, :], A1[:, j, :], ALU.mult))
                    L(dve.tensor_reduce(ss[:, 8 * j:8 * j + 8], tmp.rearrange("p (h n) -> p h n", h=8), AX_X, ALU.add))

                for i in range(16):
                    dve.wait_ge(ex, 2 * i + 2)
                    L(dve.reciprocal(stat[:, i, 6:8], stat[:, i, 2:4]))
                    L(dve.tensor_scalar(stat[:, i, 7:8], stat[:, i, 7:8], lamb[:, 5:6], None, ALU.mult))
                    e0, e1 = E[i % 2][:, 0, :], E[i % 2][:, 1, :]
                    L(dve.tensor_scalar(e0, e0, stat[:, i, 6:7], None, ALU.mult))
                    dve.scalar_tensor_tensor(out=e1, in0=e1, scalar=stat[:, i, 7:8], in1=e0, op0=ALU.mult, op1=ALU.add).then_inc(pr, 1)
                    if i + 2 < 16:
                        maxima(i + 2)
                    if i >= 2:
                        head_out(i - 2)
                    if i == 12:
                        squares(0)
                head_out(14)
                head_out(15)
                squares(1)
                dve.tensor_copy(small[:, 104:105], eps[:]).then_inc(fin, 1)
                dve.wait_ge(fin, 2)
                L(dve.reciprocal(rstd, std))
                for j in range(2):
                    v = A1[:, j, :].rearrange("p (h n) -> p h n", h=8)
                    L(dve.tensor_tensor(v, v, bc(rstd[:, 8 * j:8 * j + 8].unsqueeze(2), [P, 8, DDV]), ALU.mult))

    def under_output0(sp):
        load_expert(sp, 0, 0, 0, 0, GATE_UP)
        load_expert(sp, 0, 1, 1, 0)

    def under_norm0(sp):
        load_expert(sp, 0, 0, 0, 0, DOWN)

    def under_route0(sp):
        load_expert(sp, 0, 2, 2, 0)

    def first_chunks(sp):
        for n in range(AT[("d_in", 2)], AT[("d_in", 2)] + NW):
            load_chunk(sp, n)

    def under_output1(sp):
        load_expert(sp, 1, 1, 1, N_OF[1], GATE_UP)

    def under_norm1(sp):
        load_expert(sp, 1, 1, 1, N_OF[1], DOWN)

    def under_route1(sp):
        load_expert(sp, 1, 2, 2, N_OF[2], range(2, 6))

    setup()
    norm(0, 0, ALL, hT)
    mlstm_project()
    mlstm_attend()
    output(0, ALL, O, lambda k: vT[:, 2, OUTG + k:OUTG + k + 1], "m_out", under_output0)
    norm(0, 1, ALL, h2T, under_norm0)
    route(0, ALL, under_route0)
    experts(0)
    combine(0, ALL, first_chunks)
    norm(1, 0, ALL, hT)
    diff_project()
    diff_attend()
    output(1, LAT, A1, lambda k: small[:, 28:29], "d_out", under_output1)
    norm(1, 1, LAT, h2T, under_norm1)
    route(1, LAT, under_route1)
    experts(1)
    combine(1, LAT)
    stack.close()


_INS = ["x", "c", "ctx", "c_ctx", "ada_w", "ada_b", "norm1_g", "norm2_g", "m_w_in", "m_conv_w", "m_conv_b", "m_gate_b",
        "m_out_g", "m_w_out", "d_w_in", "d_q_g", "d_k_g", "d_lq1", "d_lk1", "d_lq2", "d_lk2", "d_sub_g", "d_w_out",
        "r_grp_w", "r_grp_b", "r_exp_w", "r_exp_b", "e_w_gu", "e_w_dn"]
_OUT = (1, NLAT, D)


def rope_constants():
    import numpy as np
    grid_w, freqs = 64, DDH // 4
    inv = (np.float32(10000.0) ** (-np.arange(freqs, dtype=np.float32) / np.float32(freqs))).astype(np.float32)
    t = np.arange(NLAT)
    place = np.stack([t // grid_w, t % grid_w], -1).astype(np.float32)
    ang = (place[..., None] * inv).reshape(NLAT, 2 * freqs)
    cs = np.zeros((TOK, 2, 2 * freqs), np.float32)
    cs[:, 0] = 1.0
    cs[NCTX:, 0] = np.cos(ang)
    cs[NCTX:, 1] = np.sin(ang)
    return np.ascontiguousarray(cs.reshape(TILES, P, 2, 2 * freqs).transpose(1, 0, 2, 3))


def kernel(**inputs):
    import numpy as _np
    import concourse.bacc as _bacc
    from concourse import mybir as _mybir
    from concourse.bass_utils import run_bass_kernel_spmd as _run

    nc = _bacc.Bacc("TRN2", target_bir_lowering=False, num_devices=1, dynamic_dma_scratch_size=8192)
    arrays, args = {}, []
    given = {n: _np.ascontiguousarray(inputs[n]) for n in _INS}
    given["rope"] = rope_constants()
    for name, a in given.items():
        arrays[f"in_{name}_dram"] = a
        args.append(nc.dram_tensor(f"in_{name}_dram", a.shape, _mybir.dt.from_np(a.dtype), kind="ExternalInput").ap())
    out = nc.dram_tensor("out_0_dram", _OUT, _mybir.dt.float32, kind="ExternalOutput").ap()
    hybrid_backbone(nc, *args, out)
    r = _run(nc, [arrays], core_ids=[0])
    return r.results[0]["out_0_dram"]
```

```python
import math
from contextlib import ExitStack

import concourse.bass as bass
from concourse import mybir
from concourse.alu_op_type import AluOpType as ALU

F32 = mybir.dt.float32
F32R = mybir.dt.float32r
I32 = mybir.dt.int32
U32 = mybir.dt.uint32
ACT = mybir.ActivationFunctionType
AX_X = mybir.AxisListType.X

P = 128
D = 1024
KT = D // P
NCTX, NLAT = 256, 256
TOK = NCTX + NLAT
TILES = TOK // P
LAT = [2, 3]
ALL = [0, 1, 2, 3]
HALF = 512
EPS = 1e-6
NEG = -1e30

MH, MDH = 4, 256
DH, DDH, DDV = 8, 64, 128
LAMBDA_INIT = 0.8 - 0.6 * math.exp(-0.3)

NG, NPG = 4, 8
NE = NG * NPG
DE = 512
B = 32
NBMAX = TOK // B
TMAX = NE + 2 * TOK // B
XROWS = (TMAX + 1) * B

GU, DN = KT * D, DE // P * D
SLOT = GU + DN
WCH = KT * HALF
PLACE = {"a": 0, "b": WCH, "c": GU, "g": SLOT, "d": SLOT + WCH, "e": SLOT + GU, "h": 2 * SLOT, "w0": 2 * SLOT + WCH,
         "w1": 2 * SLOT + GU, "x": 3 * SLOT}
X_AT = 3 * SLOT + WCH
ARENA = X_AT + TILES * D

M_ADA = [[("ada", 0, 4 + 3 * j + z) if 3 * j + z < 8 else ("ada", 1, 3 * j + z - 8) for z in range(3)]
         for j in range(4)] + [[]] * 4
_d = [("ada", 1, 4 + n) for n in range(8)]
D_ADA = [_d[0:1], _d[1:3], _d[3:4], [], _d[4:6], _d[6:8]]
D_ORDER = [2, 3, 0, 1, 4, 5]
_to = {("ada", 0, c): to for c, to in enumerate(("w0", "w1", "c", "e"))}
_order = list(_to) + [("m_in", 0)]
for _j in range(8):
    _next = [("m_in", _j + 1)] if _j < 7 else []
    _order += M_ADA[_j][:2] + _next + M_ADA[_j][2:]
_to.update({key: ("w0", "w1")[n % 2] for n, key in enumerate(sum(M_ADA, []))})
_to.update({("m_in", j): "ab"[j % 2] for j in range(8)})
_order += [("m_out", 0), ("m_out", 1), ("d_in", 2), _d[0], ("d_in", 3), ("d_in", 0), _d[1], ("d_in", 1), _d[2], _d[3],
           ("d_in", 4), _d[4], ("d_in", 5), *_d[5:], ("d_out", 0), ("d_out", 1)]
_to.update({key: "w1" for key in _d})
_to.update({("d_in", c): to for c, to in zip(D_ORDER, "abdaba")})
_to.update({(kind, n): ("w0", "w1")[n] for kind in ("m_out", "d_out") for n in range(2)})
STREAM = _order
STREAM_TO = [_to[key] for key in STREAM]
M_HIGH = ["c", "e", "c", "e", "c", "w0", "w1", "w0"]
D_HIGH = ["c", "w0", "c", "w0", "c", "w0"]
OUT_HIGH = [["g", "c"], ["h", "e"]]
AT = {key: n for n, key in enumerate(STREAM)}
SETUP_CHUNKS, COMBINE_CHUNKS = 8, 3
ADA = [n for n, key in enumerate(STREAM) if key[0] == "ada"]


class Chain:

    def __init__(self, sem):
        self.sem, self.n = sem, 0

    def link(self, eng, ins):
        ins.then_inc(self.sem, 1)
        self.n += 1
        eng.wait_ge(self.sem, self.n)


def bc(ap, shape):
    return ap.to_broadcast(shape)


def hybrid_backbone(nc, x, c, ctx, c_ctx, ada_w, ada_b, norm1_g, norm2_g, m_w_in, m_conv_w,
                    m_conv_b, m_gate_b, m_out_g, m_w_out, d_w_in, d_q_g, d_k_g, d_lq1, d_lk1,
                    d_lq2, d_lk2, d_sub_g, d_w_out, r_grp_w, r_grp_b, r_exp_w, r_exp_b,
                    e_w_gu, e_w_dn, rope, out):
    stack = ExitStack()
    sb = lambda name, shape, dt=F32: stack.enter_context(nc.sbuf_tensor(name, shape, dt))
    own = []

    def sem(name):
        if not own:
            return stack.enter_context(nc.semaphore(name))
        own[-1].append(nc.alloc_semaphore(name=name))
        return own[-1][-1]

    def phase(build_phase):
        def built(*args):
            own.append([])
            build_phase(*args)
            multiplied.clear()
            nc.clear_and_free_semaphores(own.pop())
            nc.all_engine_barrier()
        return built

    base = -(-nc.sbuf_base // 32) * 32
    arena = sb("arena", [P, ARENA])
    places_r = [nc.alloc_sbuf_tensor_at(f"place{i}_r", [P, WCH], F32R, offset=base + 4 * WCH * i)
                for i in range(ARENA // WCH)]

    def rounded(ap):
        (_, parts), *free = ap.ap
        return bass.AP(tensor=places_r[ap.offset // WCH], offset=ap.offset % WCH, ap=[[WCH, parts], *free])

    bank = [stack.enter_context(nc.psum_tensor(f"bank{i}", [P, HALF], F32)) for i in range(8)]

    def region(at, *shape):
        n = math.prod(shape)
        v = arena[:, at:at + n]
        if len(shape) == 2:
            v = v.rearrange("p (a b) -> p a b", a=shape[0])
        elif len(shape) == 3:
            v = v.rearrange("p (a b c) -> p a b c", a=shape[0], b=shape[1])
        return v

    gu_w = [region(s * SLOT, KT, D) for s in range(3)]
    dn_w = [region(s * SLOT + GU, DE // P, D) for s in range(3)]
    place = {name: region(at, KT, HALF) for name, at in PLACE.items()}
    X = region(X_AT, TILES, D)
    hT = region(PLACE["h"], KT, TOK)
    hL = region(PLACE["x"], KT, TOK)
    h2T = region(PLACE["x"], KT, TOK)

    S1 = sb("S1", [P, 2, D])
    S2 = sb("S2", [P, 2, D + 16])
    MASK = sb("MASK", [P, 3, HALF])
    ident = sb("ident", [P, P])
    upto = sb("upto", [P, P])
    after = sb("after", [P, P])
    before = sb("before", [P, P])
    ones = sb("ones", [P, P])
    veca, vecb, vecc = (region(SLOT + i * P, P) for i in range(3))
    rowv = region(SLOT + 3 * P, HALF)[0:1, :]
    vT = sb("vT", [P, 3, P])
    modT = sb("modT", [P, 2, 6 * KT, 2])
    rw = sb("rw", [P, KT, 64])
    rowb = sb("rowb", [P, HALF])
    sc = sb("sc", [P, KT, 32])
    small = sb("small", [P, 896])
    eps = sb("eps", [P, 1])
    iot = sb("iot", [P, 96], I32)
    iof = sb("iof", [P, 96])
    tab = sb("tab", [1, 2 * NE + 1], I32)
    pos = sb("pos", [P, 2, TILES], I32)
    gat = sb("gat", [P, 2, TILES])

    xs = nc.dram_tensor("xs", (XROWS, D), F32, kind="Internal").ap()
    ys = nc.dram_tensor("ys", (XROWS, D), F32, kind="Internal").ap()
    tabd = nc.dram_tensor("tabd", (2, 2 * NE + 1), I32, kind="Internal").ap()

    G = S2[:, :, 0:D]
    MASK_ROW = MASK[:].rearrange("p a b -> p (a b)")[:, 0:D]
    GATE_B, GRP, QG, KG, LQ = 0, 16, 88, 152, 216
    NROW = LQ + 4 * DDH
    N1G, N2G, CONVB, CONVW = 0, 16, 32, 48
    OUTG, CVEC, CCTX, SUBG = 0, 8, 16, 24

    w_loaded = {to: sem(f"w_loaded_{to}") for to in sorted(set(STREAM_TO))}
    multiplied = {}
    gu_loaded = [[sem(f"gu_loaded{s}_{b}") for b in range(2)] for s in range(3)]
    dn_loaded = [[sem(f"dn_loaded{s}_{b}") for b in range(2)] for s in range(3)]
    rw_loaded, gates_loaded = sem("rw_loaded"), sem("gates_loaded")

    WSRC = {"m_in": m_w_in[0], "m_out": m_w_out[0], "d_in": d_w_in[0], "d_out": d_w_out[0]}

    def load_chunk(eng, n):
        kind, *at = STREAM[n]
        src = ada_w[at[0]] if kind == "ada" else WSRC[kind]
        src = src[:, at[-1] * HALF:(at[-1] + 1) * HALF].rearrange("(k p) n -> p k n", p=P)
        before = [m for m in range(n) if STREAM_TO[m] == STREAM_TO[n]]
        if before and before[-1] in ADA:
            eng.wait_ge(ada_mm, ADA.index(before[-1]) + 1)
        elif before and before[-1] in multiplied:
            eng.wait_ge(*multiplied[before[-1]])
        eng.dma_start(place[STREAM_TO[n]], src).then_inc(w_loaded[STREAM_TO[n]], 16)

    def chunk(eng, n):
        to = STREAM_TO[n]
        eng.wait_ge(w_loaded[to], 16 * STREAM_TO[:n + 1].count(to))
        return place[to]

    def cut_high(dve, high, full):
        return dve.tensor_copy(rounded(high), full)

    def cut_low(dve, full, high):
        return dve.tensor_tensor(rounded(full), full, rounded(high).bitcast(F32), ALU.subtract)

    def multiply3(pe, to, lhs, rhs, start, stop):
        (lh, ll), (rh, rl) = [[rounded(v) for v in pair] for pair in (lhs, rhs)]
        pe.matmul(to, lh, rl, start=start, stop=False)
        pe.matmul(to, ll, rh, start=False, stop=False)
        return pe.matmul(to, lh, rh, start=False, stop=stop)

    def cut_quarters(dve, n, high, quarters, behind, done):
        full = chunk(dve, n)
        if behind:
            dve.wait_ge(*behind)
        for q, count in quarters:
            ks = slice(2 * q, 2 * q + 2)
            cut_high(dve, high[:, ks, :], full[:, ks, :]).then_inc(done, 1)
            dve.wait_ge(done, 2 * count + 1)
            cut_low(dve, full[:, ks, :], high[:, ks, :]).then_inc(done, 1)

    def load_rw(eng, layer):
        with nc.allow_non_contiguous_dma(reason="narrow router weights"):
            eng.dma_start(rw[:, :, 0:NG], r_grp_w[layer].rearrange("(k p) n -> p k n", p=P)).then_inc(rw_loaded, 16)
            eng.dma_start(rw[:, :, NG:NG + NE], r_exp_w[layer].rearrange("(k p) n -> p k n", p=P)).then_inc(rw_loaded, 16)

    ada_mm, ada_cp, ada_tr, ada_part, ada_out = (sem(f"ada_{n}") for n in ("mm", "copied", "turned", "half", "out"))
    adas = small[:, 384:896].rearrange("p (b n) -> p b n", b=2)

    def ada_multiply(pe, n):
        i = ADA.index(n)
        w = chunk(pe, n)
        if i:
            pe.wait_ge(ada_cp, i)
        for k in range(0, KT, 2):
            for q in range(4):
                kk, hf = k + q // 2, q % 2
                last = pe.matmul(bank[6][32 * q:32 * q + 32, 0:256], sc[:, kk, :], w[:, kk, hf * 256:(hf + 1) * 256],
                                 start=(k == 0), stop=(k == KT - 2), skip_group_check=True)
        last.then_inc(ada_mm, 1)

    def ada_turn(pe, n):
        i = ADA.index(n)
        pe.wait_ge(ada_cp, i + 1)
        if i:
            pe.wait_ge(ada_out, i)
        for j in range(2):
            last = pe.transpose(bank[7][:, j * P:(j + 1) * P], adas[:, i % 2, j * P:(j + 1) * P], ident[:])
        last.then_inc(ada_tr, 1)

    def ada_copy(dve, n):
        i = ADA.index(n)
        dve.wait_ge(ada_mm, i + 1)
        if i >= 2:
            dve.wait_ge(ada_tr, i - 1)
        dve.tensor_copy(adas[:, i % 2, :], bank[6][:, 0:256]).then_inc(ada_cp, 1)

    def ada_finish(dve, n):
        i = ADA.index(n)
        _, layer, ci = STREAM[n]
        dve.wait_ge(ada_tr, i + 1)
        turned = bank[7][:, 0:256].rearrange("p (j a h s) -> p a j h s", j=2, a=2, h=2)
        cols = slice(ci * 4, ci * 4 + 4)
        to = modT[:, layer, cols, :].rearrange("p (h j) s -> p j h s", h=2)
        bias = vT[:, 0, layer * 48 + ci * 4:layer * 48 + ci * 4 + 4].rearrange("p (h j) -> p j h", h=2).unsqueeze(3)
        dve.tensor_tensor(to, turned[:, 0, :, :, 0:2], bc(bias, [P, 2, 2, 2]), ALU.add).then_inc(ada_part, 1)
        dve.wait_ge(ada_part, i + 1)
        dve.tensor_tensor(to, to, turned[:, 1, :, :, 0:2], ALU.add).then_inc(ada_out, 1)

    row_ss, row_std, row_rstd = small[:, 16:20], small[:, 20:24], small[:, 24:28]

    def row_squares(act, i, t, junk, squares):
        if i:
            act.wait_ge(squares, i)
        act.activation(junk, X[:, t, :], ACT.Square, accum_out=row_ss[:, i:i + 1]).then_inc(squares, 1)

    def row_roots(act, nt, squares, std):
        act.wait_ge(squares, nt)
        act.activation(row_std[:, 0:nt], row_ss[:, 0:nt], ACT.Sqrt, bias=eps[:], scale=1.0 / D).then_inc(std, 1)

    def row_inverses(dve, nt, std):
        dve.wait_ge(std, 1)
        dve.reciprocal(row_rstd[:, 0:nt], row_std[:, 0:nt]).then_inc(std, 1)

    @phase
    def setup():
        vec, rowl, xl, const, vt_t, vt_r, rb, scr = (sem(f"setup_{n}") for n in (
            "vec", "row", "x", "const", "turned", "columns", "rows", "silu"))
        squares, std, rowp = sem("setup_squares"), sem("setup_std"), sem("setup_row_by_pool")
        rows = [(GATE_B, m_gate_b)]
        for layer in range(2):
            rows += [(GRP + 36 * layer, r_grp_b[layer:layer + 1, :]), (GRP + 36 * layer + NG, r_exp_b[layer:layer + 1, :])]
        rows += [(QG, d_q_g), (KG, d_k_g), (LQ, d_lq1), (LQ + DDH, d_lk1), (LQ + 2 * DDH, d_lq2), (LQ + 3 * DDH, d_lk2)]
        with nc.Block() as block:
            @block.sync
            def _(sp):
                sp.dma_start(X[:, 0:2, :], ctx[0].rearrange("(t p) d -> p t d", p=P)).then_inc(xl, 16)
                sp.dma_start(X[:, 2:4, :], x[0].rearrange("(t p) d -> p t d", p=P)).then_inc(xl, 16)
                sp.dma_start(vecc[0:8, :], m_out_g[0].rearrange("(r p) -> r p", p=P)).then_inc(vec, 16)
                sp.dma_start(vecc[8:16, :], c[0].rearrange("(r p) -> r p", p=P)).then_inc(vec, 16)
                sp.dma_start(vecc[16:24, :], c_ctx.rearrange("(r p) -> r p", p=P)).then_inc(vec, 16)
                sp.dma_start(vecc[24:25, :], d_sub_g).then_inc(vec, 16)
                sp.dma_start(veca[0:96, :], ada_b.rearrange("l (r p) -> (l r) p", p=P)).then_inc(vec, 16)
                for n in range(SETUP_CHUNKS):
                    load_chunk(sp, n)

            @block.scalar
            def _(act):
                act.dma_start(vecb[0:16, :], norm1_g.rearrange("l (r p) -> (l r) p", p=P)).then_inc(vec, 16)
                act.dma_start(vecb[16:32, :], norm2_g.rearrange("l (r p) -> (l r) p", p=P)).then_inc(vec, 16)
                act.dma_start(vecb[32:48, :], m_conv_b[0].rearrange("(r p) -> r p", p=P)).then_inc(vec, 16)
                act.dma_start(vecb[48:128, :], m_conv_w[0].rearrange("j (r p) -> (j r) p", p=P)).then_inc(vec, 16)
                for at, src in rows[:6]:
                    act.dma_start(rowv[0:1, at:at + src.shape[1]], src).then_inc(rowl, 16)
                act.wait_ge(vt_r, 3)
                act.activation(sc[:, :, 0], vT[:, 2, CCTX:CCTX + KT], ACT.Silu).then_inc(scr, 1)
                act.activation(sc[:, :, 1], vT[:, 2, CVEC:CVEC + KT], ACT.Silu).then_inc(scr, 1)
                act.wait_ge(scr, 3)
                act.wait_ge(xl, 32)
                for t in ALL:
                    row_squares(act, t, t, S2[:, 0, 0:D], squares)
                row_roots(act, TILES, squares, std)

            @block.gpsimd
            def _(pool):
                pool.memset(ones[:], 1.0).then_inc(const, 1)
                pool.memset(MASK[:], 0.0).then_inc(const, 1)
                pool.wait_ge(const, 2)
                sel = lambda o, i, op, cm, st, fill: pool.affine_select(
                    out=o, in_=i, compare_op=op, fill=fill, base=0, pattern=[[st, P]], channel_multiplier=cm)
                sel(ident[:], ones[:], ALU.is_equal, 1, -1, 0.0).then_inc(const, 1)
                sel(upto[:], ones[:], ALU.is_ge, -1, 1, 0.0).then_inc(const, 1)
                sel(after[:], ones[:], ALU.is_ge, 1, -1, 0.0).then_inc(const, 1)
                sel(before[:], ones[:], ALU.is_gt, -1, 1, 0.0).then_inc(const, 1)
                sel(MASK[:, 0, 3 * P:4 * P], MASK[:, 0, 3 * P:4 * P], ALU.is_ge, 1, -1, NEG).then_inc(const, 1)
                sel(MASK[:, 1, 2 * P:3 * P], MASK[:, 1, 2 * P:3 * P], ALU.is_ge, -1, 1, NEG).then_inc(const, 1)
                sel(MASK[:, 2, 3 * P:4 * P], MASK[:, 2, 3 * P:4 * P], ALU.is_ge, -1, 1, NEG).then_inc(const, 1)
                pool.memset(MASK[:, 2, 2 * P:3 * P], NEG).then_inc(const, 1)
                pool.iota(iot[:, 0:NE], pattern=[[-1, NE]], base=NE, channel_multiplier=0).then_inc(const, 1)
                pool.iota(iot[:, NE:NE + NBMAX], pattern=[[B, NBMAX]], base=B, channel_multiplier=0).then_inc(const, 1)
                for at, src in rows[6:]:
                    pool.dma_start(rowv[0:1, at:at + src.shape[1]], src).then_inc(rowp, 16)
                pool.wait_ge(scr, 3)
                with nc.allow_non_contiguous_dma(reason="narrow gate weights"):
                    pool.dma_start(rw[:, :, 0:16], m_w_in[0][:, 4 * D:4 * D + 16].rearrange("(k p) n -> p k n", p=P)).then_inc(gates_loaded, 16)

            @block.vector
            def _(dve):
                dve.memset(eps[:], EPS).then_inc(scr, 1)
                dve.memset(sc[:], 0.0).then_inc(scr, 1)
                dve.memset(rw[:], 0.0).then_inc(scr, 1)
                dve.wait_ge(const, 12)
                dve.tensor_copy(iof[:, 0:NE + NBMAX], iot[:, 0:NE + NBMAX]).then_inc(scr, 1)
                dve.wait_ge(scr, 4)
                dve.wait_ge(vt_t, 3)
                dve.tensor_copy(vT[:, 0, 0:96], bank[0][:, 0:96]).then_inc(vt_r, 1)
                dve.tensor_copy(vT[:, 1, :], bank[0][:, 128:256]).then_inc(vt_r, 1)
                dve.tensor_copy(vT[:, 2, 0:25], bank[0][:, 256:281]).then_inc(vt_r, 1)
                for n in range(4):
                    ada_copy(dve, n)
                    if n:
                        ada_finish(dve, n - 1)
                    if n == 2:
                        row_inverses(dve, TILES, std)
                ada_finish(dve, 3)
                dve.wait_ge(vt_t, 4)
                dve.tensor_copy(rowb[:, 0:NROW], bank[1][:, 0:NROW]).then_inc(rb, 1)

            @block.tensor
            def _(pe):
                pe.wait_ge(const, 3)
                pe.wait_ge(vec, 16 * 9)
                pe.transpose(bank[0][:, 0:96], veca[0:96, :], ident[0:96, 0:96]).then_inc(vt_t, 1)
                pe.transpose(bank[0][:, 128:256], vecb[:], ident[:]).then_inc(vt_t, 1)
                pe.transpose(bank[0][:, 256:281], vecc[0:25, :], ident[0:25, 0:25]).then_inc(vt_t, 1)
                pe.wait_ge(scr, 6)
                for n in range(4):
                    ada_multiply(pe, n)
                    if n:
                        ada_turn(pe, n - 1)
                ada_turn(pe, 3)
                pe.wait_ge(rowl, 16 * 6)
                pe.wait_ge(rowp, 16 * (len(rows) - 6))
                pe.matmul(bank[1][:, 0:NROW], ones[0:1, :], rowv[0:1, 0:NROW], start=True, stop=True).then_inc(vt_t, 1)

    @phase
    def norm(layer, which, tiles, dst, extra_sync=None, high=None):
        g = vT[:, 1, (N1G, N2G)[which] + KT * layer:(N1G, N2G)[which] + KT * (layer + 1)].unsqueeze(2)
        shift = modT[:, layer, 24 * which:24 * which + KT, :]
        scale = modT[:, layer, 24 * which + KT:24 * which + 2 * KT, :]
        A = small[:, 0:16].rearrange("p (k s) -> p k s", k=KT)
        nt = len(tiles)
        a_, xn, xa, tr, ev, cut = (sem(f"norm{layer}{which}_{n}") for n in (
            "scale", "rows", "rows_by_scalar", "turned", "out", "cut"))
        rows = [S1[:, 0, :], S1[:, 1, :], G[:, 0, :], G[:, 1, :]]
        with nc.Block() as block:
            @block.sync
            def _(sp):
                if extra_sync:
                    extra_sync(sp)

            @block.scalar
            def _(act):
                for i in range(2, nt):
                    act.activation(rows[i], X[:, tiles[i], :], ACT.Copy, scale=row_rstd[:, i:i + 1]).then_inc(xa, 1)
                act.wait_ge(a_, 1)
                for si in range(nt // 2):
                    s = tiles[2 * si] // 2
                    for k in range(KT) if high is not None else (2, 3, 6, 7):
                        act.wait_ge(tr, KT * si + 2 * (k // 2) + 2)
                        act.activation(dst[:, k, 256 * s:256 * s + 256], bank[4 * si + k // 2][:, 256 * (k % 2):256 * (k % 2) + 256], ACT.Identity,
                                       bias=shift[:, k, s:s + 1], scale=A[:, k, s:s + 1]).then_inc(ev, 1)

            @block.vector
            def _(dve):
                dve.scalar_tensor_tensor(out=A, in0=scale, scalar=1.0, in1=bc(g, [P, KT, 2]), op0=ALU.add,
                                         op1=ALU.mult).then_inc(a_, 1)
                for i in range(2):
                    dve.tensor_scalar(rows[i], X[:, tiles[i], :], row_rstd[:, i:i + 1], None, ALU.mult).then_inc(xn, 1)
                dve.wait_ge(a_, 1)
                for si in range(nt // 2):
                    s = tiles[2 * si] // 2
                    for k in range(0, KT, 2) if high is not None else ():
                        dve.wait_ge(ev, KT * si + k + 2)
                        cols = slice(256 * s, 256 * s + 256)
                        cut_high(dve, high[:, k:k + 2, cols], dst[:, k:k + 2, cols]).then_inc(cut, 1)
                        dve.wait_ge(cut, (KT * si + k) + 1)
                        cut_low(dve, dst[:, k:k + 2, cols], high[:, k:k + 2, cols]).then_inc(cut, 1)
                    for k in (0, 1, 4, 5) if high is None else ():
                        dve.wait_ge(tr, KT * si + 2 * (k // 2) + 2)
                        dve.tensor_scalar(dst[:, k, 256 * s:256 * s + 256], bank[4 * si + k // 2][:, 256 * (k % 2):256 * (k % 2) + 256],
                                          A[:, k, s:s + 1], shift[:, k, s:s + 1], ALU.mult, ALU.add).then_inc(ev, 1)

            @block.tensor
            def _(pe):
                for si in range(nt // 2):
                    pe.wait_ge((xn, xa)[si], 2)
                    for k in range(KT):
                        for j in range(2):
                            last = pe.transpose(bank[4 * si + k // 2][:, (k % 2) * 256 + j * P:(k % 2) * 256 + (j + 1) * P],
                                                rows[2 * si + j][:, k * P:(k + 1) * P], ident[:])
                        last.then_inc(tr, 1)

    qkT = region(SLOT, 2 * KT, TOK)
    V = region(SLOT + GU, TILES, D)
    O = region(GU, TILES, D)
    Fg = small[:, 32:64].rearrange("p (t c) -> p t c", t=TILES)
    ag = small[:, 64:96].rearrange("p (t c) -> p t c", t=TILES)

    @phase
    def mlstm_project():
        padv = [S2[:, b, 0:520].rearrange("p (s n) -> p s n", s=2) for b in range(2)]
        accv = [S2[:, b, 520:520 + 512].rearrange("p (s n) -> p s n", s=2) for b in range(2)]
        lf = small[:, 96:128].rearrange("p (t c) -> p t c", t=TILES)
        g16 = small[:, 128:192].rearrange("p (t c) -> p t c", t=TILES)
        af, ex, ln = (small[:, a:a + 32].rearrange("p (t c) -> p t c", t=TILES) for a in (192, 224, 256))
        fu = small[:, 288:384].rearrange("p (w t c) -> p w t c", w=3, t=TILES)
        gmm, gdv, gac, fmm, done = (sem(f"gates_{n}") for n in ("mm", "vector", "scalar", "sums", "done"))
        unit, ev, padz, cv, si_, chain = (sem(f"mproj_{n}") for n in ("unit", "evacuated", "pads", "conv", "silu", "chain"))
        grow = sem("mproj_gate_rows")
        NU = 32
        split = sem("mproj_cut")
        high = [place[to] for to in M_HIGH]
        multiplied.update({AT[("m_in", j)]: (unit, 4 * (j + 1)) for j in range(NU // 4)})
        plan = []
        for j in range(8):
            ada = [AT[key] for key in M_ADA[j]]
            plan.append(("unit", 4 * j))
            for z in range(1, 4):
                if ada:
                    plan.append(("mul", ada[z - 1]))
                plan.append(("unit", 4 * j + z))
                if ada:
                    plan.append(("turn", ada[z - 1]))

        with nc.Block() as block:
            @block.sync
            def _(sp):
                for n in range(SETUP_CHUNKS, AT[("m_out", 0)]):
                    load_chunk(sp, n)

            @block.tensor
            def _(pe):
                pe.wait_ge(gates_loaded, 16)
                for k in range(0, KT, 4):
                    for part in (hT, hL):
                        for q in range(4):
                            last = pe.matmul(bank[3][32 * q:32 * q + 32, :], rw[:, k + q, 0:32], rounded(part[:, k + q, :]).bitcast(F32),
                                             start=(k == 0 and part is hT), stop=(k == KT - 4 and part is hL), skip_group_check=True)
                last.then_inc(grow, 1)
                pe.wait_ge(grow, 2)
                for t in ALL:
                    last = pe.transpose(bank[4][:, t * P:(t + 1) * P], S1[:, 0, t * P:(t + 1) * P], ident[:])
                last.then_inc(gmm, 1)

                def one(u):
                    j, z = u // 4, u % 4
                    w, wh = place[STREAM_TO[AT[("m_in", j)]]], high[j]
                    b = bank[u % 3]
                    if u >= 3:
                        pe.wait_ge(ev, u - 2)
                    zs = slice(z * P, (z + 1) * P)
                    for k in range(KT):
                        if z == 0 and k % 2 == 0:
                            pe.wait_ge(split, 8 * j + k + 2)
                        if j < 4:
                            last = multiply3(pe, b[:], (wh[:, k, zs], w[:, k, zs]), (hT[:, k, :], hL[:, k, :]), k == 0, k == KT - 1)
                        else:
                            last = multiply3(pe, b[:], (hT[:, k, zs], hL[:, k, zs]), (wh[:, k, :], w[:, k, :]), k == 0, k == KT - 1)
                    last.then_inc(unit, 1)

                for what, n in plan:
                    if what == "unit":
                        one(n)
                        if n == 1:
                            pe.wait_ge(done, 1)
                            flat = small[:, 96:128]
                            pe.matmul(bank[4][:, 0:32], upto[:], flat, start=True, stop=True)
                            pe.matmul(bank[4][:, 32:64], after[:], flat, start=True, stop=True)
                            pe.matmul(bank[4][:, 64:96], ones[:], flat, start=True, stop=True).then_inc(fmm, 1)
                    elif what == "mul":
                        ada_multiply(pe, n)
                    else:
                        ada_turn(pe, n)

            @block.scalar
            def _(act):
                act.wait_ge(grow, 1)
                act.activation(S1[:, 0, 0:TOK], bank[3][:], ACT.Copy).then_inc(grow, 1)
                act.wait_ge(gdv, 3)
                act.activation(ex, af, ACT.Exp, scale=-1.0).then_inc(gac, 1)
                act.wait_ge(gac, 1)
                act.activation(ln, ex, ACT.Ln, bias=1.0).then_inc(gac, 1)
                act.wait_ge(padz, 2)

                def silu(m):
                    act.wait_ge(cv, m + 1)
                    act.activation(qkT[:, m, :], accv[m % 2], ACT.Silu).then_inc(si_, 1)

                for u in range(NU):
                    act.wait_ge(unit, u + 1)
                    if u < 16:
                        if u >= 2:
                            act.wait_ge(cv, u - 1)
                        act.activation(padv[u % 2][:, :, 2:258], bank[u % 3][:].rearrange("p (s n) -> p s n", s=2), ACT.Copy).then_inc(ev, 1)
                        if u >= 1:
                            silu(u - 1)
                    elif u < 24:
                        if u == 16:
                            silu(15)
                        j, z = u // 4 - 4, u % 4
                        act.activation(V[:, z, j * HALF:(j + 1) * HALF], bank[u % 3][:], ACT.Copy).then_inc(ev, 1)
                    else:
                        j, z = u // 4 - 6, u % 4
                        act.activation(O[:, z, j * HALF:(j + 1) * HALF], bank[u % 3][:], ACT.Sigmoid).then_inc(ev, 1)

            @block.vector
            def _(dve):
                ch = Chain(chain)
                def cut(j, qs):
                    earlier = [i for i in range(j) if M_HIGH[i] == M_HIGH[j]]
                    cut_quarters(dve, AT[("m_in", j)], high[j], [(q, 4 * j + q) for q in qs],
                                 (unit, 4 * (earlier[-1] + 1)) if earlier else None, split)

                cut(0, range(4))
                dve.memset(padv[0], 0.0).then_inc(padz, 1)
                dve.memset(padv[1], 0.0).then_inc(padz, 1)
                dve.wait_ge(gmm, 1)
                gp = bank[4][:].rearrange("p (t q n) -> p t n q", t=TILES, q=4)
                dve.tensor_reduce(g16, gp[:, :, 0:16, :], AX_X, ALU.add).then_inc(gdv, 1)
                dve.wait_ge(gdv, 1)
                dve.tensor_tensor(g16, g16, bc(rowb[:, GATE_B:GATE_B + 16].unsqueeze(1), [P, TILES, 16]), ALU.add).then_inc(gdv, 1)
                dve.wait_ge(gdv, 2)
                f = g16[:, :, 8:16]
                dve.scalar_tensor_tensor(out=af, in0=f, scalar=-1.0, in1=f, op0=ALU.mult, op1=ALU.max).then_inc(gdv, 1)
                dve.wait_ge(gac, 2)
                dve.scalar_tensor_tensor(out=lf, in0=f, scalar=0.0, in1=ln, op0=ALU.min, op1=ALU.subtract).then_inc(done, 1)

                def sums():
                    dve.wait_ge(fmm, 1)
                    ch.link(dve, dve.tensor_copy(small[:, 288:384], bank[4][:, 0:96]))
                    tot = lambda t, a: fu[:, 2, t, a:a + 4]
                    for t in ALL:
                        ch.link(dve, dve.tensor_copy(Fg[:, t, 0:4], fu[:, 0, t, 0:4]))
                        ch.link(dve, dve.tensor_copy(Fg[:, t, 4:8], fu[:, 1, t, 4:8]))
                    earlier = {0: [1], 1: [], 2: [0, 1, 3], 3: [0, 1]}
                    for t in ALL:
                        for o in range(t):
                            ch.link(dve, dve.tensor_tensor(Fg[:, t, 0:4], Fg[:, t, 0:4], tot(o, 0), ALU.add))
                        for o in earlier[t]:
                            ch.link(dve, dve.tensor_tensor(Fg[:, t, 4:8], Fg[:, t, 4:8], tot(o, 4), ALU.add))
                    ch.link(dve, dve.tensor_tensor(ag, g16[:, :, 0:8], Fg, ALU.subtract))

                def conv(m):
                    pd, ac = padv[m % 2], accv[m % 2]
                    col = lambda j: vT[:, 1, CONVW + j * 16 + m:CONVW + j * 16 + m + 1]
                    dve.wait_ge(ev, m + 1)
                    if m >= 2:
                        dve.wait_ge(si_, m - 1)
                    ch.link(dve, dve.tensor_scalar(ac, pd[:, :, 2:258], col(2), vT[:, 1, CONVB + m:CONVB + m + 1], ALU.mult, ALU.add))
                    for j in (0, 1, 3):
                        ch.link(dve, dve.scalar_tensor_tensor(out=ac, in0=pd[:, :, j:j + 256], scalar=col(j), in1=ac, op0=ALU.mult, op1=ALU.add))
                    dve.scalar_tensor_tensor(out=ac, in0=pd[:, :, 4:260], scalar=col(4), in1=ac, op0=ALU.mult, op1=ALU.add).then_inc(cv, 1)

                dve.wait_ge(padz, 2)
                for what, n in plan:
                    if what == "unit":
                        if n < 16:
                            conv(n)
                        if n == 17:
                            sums()
                        if n % 4 < 3 and n // 4 < 7:
                            cut(n // 4 + 1, ((0,), (1,), (2, 3))[n % 4])
                    elif what == "mul":
                        ada_copy(dve, n)
                    else:
                        ada_finish(dve, n)

    SEEN = {(0, 0): (0, 1), (1, 0): (0, 2), (2, 0): (0, 3), (3, 0): (0, 4),
            (0, 1): (0, 2), (1, 1): (1, 1), (2, 1): (0, 4), (3, 1): (0, 4)}

    def mask_of(t, d):
        n = SEEN[t, d][1]
        if d == 0:
            return MASK[:, 0, (4 - n) * P:HALF]
        if t == 3:
            return MASK[:, 2, :]
        return MASK[:, 1, {0: 2, 1: 2, 2: 0}[t] * P:({0: 2, 1: 2, 2: 0}[t] + n) * P]

    @phase
    def mlstm_attend():
        DAT, at = {}, 0
        for t in ALL:
            for d in range(2):
                DAT[t, d] = at
                at += SEEN[t, d][1] * P
        ITER = [(h, t) for h in range(MH) for t in ALL]
        N = len(ITER)
        DBUF = [PLACE[p] for p in ("h", "x", "a", "b")]
        dm = lambda h, t, d: region(DBUF[h] + DAT[t, d], SEEN[t, d][1] * P)
        big = {0: 1, 1: 0, 2: 1, 3: 1}
        M = [small[:, a:a + 8] for a in (96, 104)]
        nM = [small[:, a:a + 8] for a in (112, 120)]
        sm = [small[:, a:a + 8] for a in (128, 136)]
        gd = [small[:, a:a + 8] for a in (144, 152)]
        den = [small[:, a:a + 8] for a in (160, 168)]
        rr = [small[:, a:a + 8] for a in (176, 184)]
        ssq, std, rstd = small[:, 192:208], small[:, 208:224], small[:, 224:240]
        PT = [S1[:, b, 0:HALF] for b in range(2)]
        junk = [S1[:, b, HALF:HALF + 256] for b in range(2)]
        ab, aD, aM, ex, gu_, s_mm, td, pr, tr, pt, pv, ro, sq, fin, chain = (sem(f"matt_{n}") for n in (
            "rows", "masked", "negmax", "exp", "guard", "scores", "products", "weights", "turned", "copied",
            "heads", "gated", "squares", "final", "chain"))
        zero, filled = sem("matt_zero"), sem("matt_filled")
        with nc.Block() as block:
            @block.gpsimd
            def _(pool):
                pool.memset(G[:, 0, :], 0.0).then_inc(zero, 1)

            @block.sync
            def _(sp):
                load_chunk(sp, AT[("m_out", 0)])
                load_chunk(sp, AT[("m_out", 1)])
                sp.wait_ge(zero, 1)
                for dram in (xs, ys):
                    sp.dma_start(dram[0:TMAX * B, :].rearrange("(n p) d -> p n d", p=P),
                                 bc(G[:, 0:1, :], [P, TMAX * B // P, D])).then_inc(filled, 16)
                sp.dma_start(xs[TMAX * B:XROWS, :], G[0:B, 0, :]).then_inc(filled, 16)
                sp.wait_ge(filled, 48)

            @block.tensor
            def _(pe):
                def rows(h):
                    if h:
                        pe.wait_ge(aD, h)
                    for d in range(2):
                        for t in ALL:
                            last = pe.matmul(bank[d][:, t * P:(t + 1) * P], bc(ag[:, t, 4 * d + h:4 * d + h + 1], [P, P]),
                                             ident[:], start=True, stop=True)
                    last.then_inc(ab, 1)

                def scores(h, t):
                    i = 4 * h + t
                    n = 256 if t < 2 else 512
                    if i >= 2:
                        pe.wait_ge(td, i - 1)
                    for kk in range(2):
                        last = pe.matmul(bank[2 + i % 2][:, 0:n], qkT[:, 2 * h + kk, t * P:(t + 1) * P],
                                         qkT[:, 8 + 2 * h + kk, 0:n], start=(kk == 0), stop=(kk == 1))
                    last.then_inc(s_mm, 1)

                def turn(h, t):
                    i = 4 * h + t
                    pe.wait_ge(pr, i + 1)
                    if i >= 2:
                        pe.wait_ge(pt, i - 1)
                    n = SEEN[t, big[t]][1]
                    for s in range(n):
                        last = pe.transpose(bank[4 + i % 2][:, s * P:(s + 1) * P], dm(h, t, big[t])[:, s * P:(s + 1) * P], ident[:])
                    last.then_inc(tr, 1)

                def heads(h, t):
                    i = 4 * h + t
                    pe.wait_ge(pt, i + 1)
                    if i >= 2:
                        pe.wait_ge(ro, i - 1)
                        pe.wait_ge(sq, i - 1)
                    k0, n = SEEN[t, big[t]]
                    for s in range(n):
                        last = pe.matmul(bank[6 + i % 2][:, 0:MDH], PT[i % 2][:, s * P:(s + 1) * P],
                                         V[:, k0 + s, h * MDH:(h + 1) * MDH], start=(s == 0), stop=(s == n - 1))
                    last.then_inc(pv, 1)

                rows(0)
                rows(1)
                scores(0, 0)
                scores(0, 1)
                for i, (h, t) in enumerate(ITER):
                    if t == 0 and h + 2 < MH:
                        rows(h + 2)
                    if i + 2 < N:
                        scores(*ITER[i + 2])
                    turn(h, t)
                    if i:
                        heads(*ITER[i - 1])
                heads(*ITER[N - 1])

            @block.vector
            def _(dve):
                ch = Chain(chain)

                def masked(h, t):
                    dve.wait_ge(ab, h + 1)
                    for d in range(2):
                        k0, n = SEEN[t, d]
                        last = dve.tensor_tensor_reduce(dm(h, t, d), bank[d][:, k0 * P:(k0 + n) * P], mask_of(t, d),
                                                        1.0, 0.0, ALU.add, ALU.max, M[h % 2][:, 2 * t + d:2 * t + d + 1])
                    if t == 3:
                        last.then_inc(aD, 1)
                        dve.wait_ge(aD, h + 1)
                        dve.tensor_scalar(nM[h % 2], M[h % 2], -1.0, None, ALU.mult).then_inc(aM, 1)
                        fv = small[:, 32:64].rearrange("p (t d h) -> p t d h", t=TILES, d=2)[:, :, :, h]
                        dve.tensor_tensor(sm[h % 2].rearrange("p (t d) -> p t d", d=2), M[h % 2].rearrange("p (t d) -> p t d", d=2),
                                          fv, ALU.add).then_inc(aM, 1)

                def weights(h, t):
                    i = 4 * h + t
                    dve.wait_ge(s_mm, i + 1)
                    dve.wait_ge(ex, 2 * i + 2)
                    both = slice(2 * t, 2 * t + 2)
                    dd, r = den[h % 2][:, both], rr[h % 2][:, both]
                    for d in range(2):
                        k0, n = SEEN[t, d]
                        v = dm(h, t, d)
                        last = dve.tensor_tensor_reduce(v, bank[2 + i % 2][:, k0 * P:(k0 + n) * P], v, MDH ** -0.5, 0.0,
                                                        ALU.mult, ALU.add, dd[:, d:d + 1])
                    last.then_inc(td, 1)
                    dve.wait_ge(td, i + 1)
                    ch.link(dve, dve.scalar_tensor_tensor(out=dd, in0=dd, scalar=-1.0, in1=dd, op0=ALU.mult, op1=ALU.max))
                    dve.wait_ge(gu_, h + 1)
                    ch.link(dve, dve.tensor_tensor(dd, dd, gd[h % 2][:, both], ALU.max))
                    ch.link(dve, dve.reciprocal(r, dd))
                    b = big[t]
                    o = 1 - b
                    kb, ko, no = SEEN[t, b][0], SEEN[t, o][0], SEEN[t, o][1]
                    whole, part = dm(h, t, b), dm(h, t, o)
                    ch.link(dve, dve.tensor_scalar(whole, whole, r[:, b:b + 1], None, ALU.mult))
                    into = whole[:, (ko - kb) * P:(ko - kb + no) * P]
                    dve.scalar_tensor_tensor(out=into, in0=part, scalar=r[:, o:o + 1], in1=into,
                                             op0=ALU.mult, op1=ALU.add).then_inc(pr, 1)

                def gated(h, t):
                    i = 4 * h + t
                    dve.wait_ge(pv, i + 1)
                    o = O[:, t, h * MDH:(h + 1) * MDH]
                    dve.tensor_tensor(o, bank[6 + i % 2][:, 0:MDH], o, ALU.mult).then_inc(ro, 1)

                for h in range(2):
                    for t in ALL:
                        masked(h, t)
                for i, (h, t) in enumerate(ITER):
                    weights(h, t)
                    if h + 2 < MH:
                        masked(h + 2, t)
                    if i >= 2:
                        gated(*ITER[i - 2])
                gated(*ITER[N - 2])
                gated(*ITER[N - 1])
                dve.wait_ge(fin, 1)
                dve.reciprocal(rstd, std).then_inc(fin, 1)
                dve.wait_ge(fin, 2)
                dve.wait_ge(ro, 16)
                for h in (0, 1, 2):
                    for t in ALL:
                        o = O[:, t, h * MDH:(h + 1) * MDH]
                        dve.tensor_scalar(o, o, rstd[:, 4 * h + t:4 * h + t + 1], None, ALU.mult).then_inc(fin, 1)

            @block.scalar
            def _(act):
                def exps(h, t):
                    act.wait_ge(aM, 2 * h + 2)
                    for d in range(2):
                        v = dm(h, t, d)
                        act.activation(v, v, ACT.Exp, bias=nM[h % 2][:, 2 * t + d:2 * t + d + 1]).then_inc(ex, 1)
                    if t == 0:
                        act.activation(gd[h % 2], sm[h % 2], ACT.Exp, scale=-1.0).then_inc(gu_, 1)

                def square(i):
                    act.wait_ge(ro, i + 1)
                    act.activation(junk[i % 2], bank[6 + i % 2][:, 0:MDH], ACT.Square, accum_out=ssq[:, i:i + 1]).then_inc(sq, 1)

                for t in ALL:
                    exps(0, t)
                for i, (h, t) in enumerate(ITER):
                    act.wait_ge(tr, i + 1)
                    if i >= 2:
                        act.wait_ge(pv, i - 1)
                    n = SEEN[t, big[t]][1] * P
                    act.activation(PT[i % 2][:, 0:n], bank[4 + i % 2][:, 0:n], ACT.Copy).then_inc(pt, 1)
                    if h + 1 < MH:
                        exps(h + 1, t)
                    if i >= 2:
                        square(i - 2)
                square(N - 2)
                square(N - 1)
                act.wait_ge(sq, 16)
                act.activation(std, ssq, ACT.Sqrt, bias=eps[:], scale=1.0 / MDH).then_inc(fin, 1)
                act.wait_ge(fin, 2)
                for t in ALL:
                    o = O[:, t, 3 * MDH:4 * MDH]
                    act.activation(o, o, ACT.Copy, scale=rstd[:, 12 + t:13 + t]).then_inc(gu_, 1)

    def gate_rows(pe, act, layer, part, streams, mm, ev):
        if pe is not None:
            for si, s in enumerate(streams):
                for hf in range(2):
                    for k in range(4):
                        last = pe.matmul(bank[2 * si + hf][:, k * P:(k + 1) * P],
                                         bc(modT[:, layer, 8 * part + 4 * hf + k, s:s + 1], [P, P]), ident[:], start=True, stop=True)
                    last.then_inc(mm, 1)
        if act is not None:
            for si, s in enumerate(streams):
                for hf in range(2):
                    act.wait_ge(mm, 2 * si + hf + 1)
                    act.activation(G[:, s, hf * HALF:(hf + 1) * HALF], bank[2 * si + hf][:], ACT.Copy).then_inc(ev, 1)

    @phase
    def output(layer, tiles, src, colv, wkey, prefetch):
        nt = len(tiles)
        streams = [0, 1] if nt == 4 else [1]
        gm, ge, tr, ev, ym, yt, ya, cl = (sem(f"out{layer}_{n}") for n in (
            "gate_mm", "gate", "turned", "columns", "product", "gated", "added", "col"))
        squares, std = sem(f"out{layer}_squares"), sem(f"out{layer}_std")
        rL = region(PLACE["x"], KT, nt * P)
        rH = region(PLACE["x"] + KT * nt * P if layer else PLACE["h"], KT, nt * P)
        cut, rcut = sem(f"out{layer}_weights_cut"), sem(f"out{layer}_heads_cut")
        high = [place[to] for to in OUT_HIGH[layer]]
        units = [(0, 0), (1, 0), (0, 1), (1, 1)] + [(j, cc) for j in range(2, nt) for cc in range(2)]
        tmp = [S1[:, b, 0:HALF] for b in range(2)]
        with nc.Block() as block:
            @block.sync
            def _(sp):
                load_rw(sp, layer)
                prefetch(sp)

            @block.tensor
            def _(pe):
                gate_rows(pe, None, layer, 2, streams, gm, ge)
                for k in range(KT):
                    if k == 4:
                        pe.wait_ge(ge, 2 * len(streams))
                    for j in range(nt):
                        last = pe.transpose(bank[(4 + k) % 8][:, j * P:(j + 1) * P], src[:, j, k * P:(k + 1) * P], ident[:])
                    last.then_inc(tr, 1)
                pe.wait_ge(ev, KT)
                for u, (j, cc) in enumerate(units):
                    w, js = place[STREAM_TO[AT[(wkey, cc)]]], slice(j * P, (j + 1) * P)
                    for k in range(KT):
                        if k % 2 == 0:
                            pe.wait_ge(cut, 8 * cc + k + 2)
                            pe.wait_ge(rcut, k + 2)
                        last = multiply3(pe, bank[u % 8][:], (rH[:, k, js], rL[:, k, js]), (high[cc][:, k, :], w[:, k, :]),
                                         k == 0, k == KT - 1)
                    last.then_inc(ym, 1)

            @block.scalar
            def _(act):
                gate_rows(None, act, layer, 2, streams, gm, ge)
                if layer:
                    act.wait_ge(cl, 1)
                for k in range(KT):
                    act.wait_ge(tr, k + 1)
                    act.activation(rL[:, k, :], bank[(4 + k) % 8][:, 0:nt * P], ACT.Copy, scale=colv(k)).then_inc(ev, 1)
                for j, t in enumerate(tiles):
                    act.wait_ge(ya, units.index((j, 1)) + 1)
                    row_squares(act, j, t, MASK_ROW, squares)
                row_roots(act, nt, squares, std)

            @block.vector
            def _(dve):
                if layer:
                    dve.tensor_scalar(small[:, 28:29], vT[:, 2, SUBG:SUBG + 1], 1.0 - LAMBDA_INIT, None, ALU.mult).then_inc(cl, 1)
                    dve.wait_ge(cl, 1)
                quarters = lambda cc: [(q, 4 * cc + q) for q in range(4)]
                cut_quarters(dve, AT[(wkey, 0)], high[0], quarters(0), None, cut)
                for k in range(0, KT, 2):
                    dve.wait_ge(ev, k + 2)
                    cut_high(dve, rH[:, k:k + 2, :], rL[:, k:k + 2, :]).then_inc(rcut, 1)
                    dve.wait_ge(rcut, k + 1)
                    cut_low(dve, rL[:, k:k + 2, :], rH[:, k:k + 2, :]).then_inc(rcut, 1)
                cut_quarters(dve, AT[(wkey, 1)], high[1], quarters(1), (tr, KT), cut)
                dve.wait_ge(ge, 2 * len(streams))
                for u, (j, cc) in enumerate(units):
                    t = tiles[j]
                    dve.wait_ge(ym, u + 1)
                    if u >= 2:
                        dve.wait_ge(ya, u - 1)
                    dve.tensor_tensor(tmp[u % 2], bank[u % 8][:], G[:, t // 2, cc * HALF:(cc + 1) * HALF], ALU.mult).then_inc(yt, 1)
                    dve.wait_ge(yt, u + 1)
                    xx = X[:, t, cc * HALF:(cc + 1) * HALF]
                    dve.tensor_tensor(xx, xx, tmp[u % 2], ALU.add).then_inc(ya, 1)
                row_inverses(dve, nt, std)

    @phase
    def route(layer, tiles, prefetch):
        nt = len(tiles)
        mask = MASK[:].rearrange("p a b -> p (a b)")
        state = {"at": 0}

        def take(*shape):
            n = math.prod(shape)
            v = mask[:, state["at"]:state["at"] + n]
            state["at"] += n
            return v.rearrange("p (t n) -> p t n", t=shape[0]) if len(shape) == 2 else v

        lg, el, eq, oh1, oh2, cnt, rk, tmp = (take(nt, 36), *(take(nt, NE) for _ in range(7)))
        gx, gq = take(nt, NG), take(nt, NG)
        m1, m2, mg, gs, e2, r, t1, t2 = (take(nt) for _ in range(8))
        tot = take(nt, NE)
        ncol, nb, base = take(1), take(1), take(NE)
        key32 = iof[:, 0:NE]
        lgt, lgc = sem(f"route{layer}_logit_rows"), sem(f"route{layer}_logit_rows_copied")
        lgm, dv, ac, cn, pm, nbd, tbm, tbd, pd, rt, re, chain = (sem(f"route{layer}_{n}") for n in (
            "logits", "vector", "scalar", "counts", "prefix", "blocks", "table_mm", "table", "pos",
            "row_turned", "row_ready", "chain"))
        sca = sem(f"route{layer}_scattered")
        rows = [S1[:, 0, :], S1[:, 1, :], G[:, 0, :], G[:, 1, :]]
        with nc.Block() as block:
            @block.sync
            def _(sp):
                prefetch(sp)

            @block.tensor
            def _(pe):
                pe.wait_ge(rw_loaded, 32 * (layer + 1))
                n, t0 = nt * P, tiles[0] * P
                for k in range(0, KT, 2):
                    for q in range(4):
                        kk, hf = k + q // 2, q % 2
                        last = pe.matmul(bank[3][32 * q:32 * q + 32, 0:n], rw[:, kk, 32 * hf:32 * hf + 32], h2T[:, kk, t0:t0 + n],
                                         start=(k == 0), stop=(k == KT - 2), skip_group_check=True)
                last.then_inc(lgt, 1)
                pe.wait_ge(lgc, 1)
                for j in range(nt):
                    last = pe.transpose(bank[0][:, j * P:(j + 1) * P], S2[:, 0, j * P:(j + 1) * P], ident[:])
                last.then_inc(lgm, 1)
                for j, t in enumerate(tiles):
                    for hf in range(2):
                        u = 2 * j + hf
                        if u >= 4:
                            pe.wait_ge(re, u - 3)
                        for k in range(4):
                            last = pe.transpose(bank[4 + u % 4][:, k * P:(k + 1) * P], h2T[:, 4 * hf + k, t * P:(t + 1) * P], ident[:])
                        last.then_inc(rt, 1)
                pe.wait_ge(cn, 1)
                flat = cnt.rearrange("p t n -> p (t n)")
                pe.matmul(bank[1][:, 0:nt * NE], before[:], flat, start=True, stop=True)
                pe.matmul(bank[1][:, 128:128 + nt * NE], ones[:], flat, start=True, stop=True)
                for j in range(nt):
                    last = pe.matmul(bank[2][0:NE, 0:P], cnt[:, j, :], ones[:], start=(j == 0), stop=(j == nt - 1))
                last.then_inc(pm, 1)
                pe.wait_ge(nbd, 2)
                pe.matmul(bank[3][:, 0:NE], bc(nb[0:NE, :], [NE, P]), ident[0:NE, 0:NE], start=True, stop=True)
                pe.matmul(bank[3][:, NE:2 * NE], bc(nb[0:NE, :], [NE, P]), before[0:NE, 0:NE], start=True, stop=True)
                pe.matmul(bank[3][:, 2 * NE:2 * NE + 1], bc(nb[0:NE, :], [NE, P]), ones[0:NE, 0:1], start=True, stop=True).then_inc(tbm, 1)

            @block.scalar
            def _(act):
                act.wait_ge(dv, 1)
                act.activation(gx, gx, ACT.Exp).then_inc(ac, 1)
                for u in range(2 * nt):
                    act.wait_ge(rt, u + 1)
                    if u == 4:
                        act.wait_ge(lgm, 1)
                    act.activation(rows[u // 2][:, (u % 2) * HALF:(u % 2 + 1) * HALF], bank[4 + u % 4][:], ACT.Copy).then_inc(re, 1)
                    if u == 3:
                        act.wait_ge(dv, 2)
                        act.activation(e2, e2, ACT.Exp).then_inc(ac, 1)

            @block.vector
            def _(dve):
                ch = Chain(chain)
                L = lambda ins: ch.link(dve, ins)
                w3 = lambda v, n: bc(v.unsqueeze(2), [P, nt, n])
                dve.wait_ge(lgt, 1)
                dve.tensor_copy(S2[:, 0, 0:nt * P], bank[3][:, 0:nt * P]).then_inc(lgc, 1)
                dve.wait_ge(lgm, 1)
                both = bank[0][:, 0:nt * P].rearrange("p (t a n) -> p t a n", t=nt, a=2)
                L(dve.tensor_copy(lg, both[:, :, 0, 0:36]))
                L(dve.tensor_tensor(lg, lg, both[:, :, 1, 0:36], ALU.add))
                L(dve.tensor_tensor(lg, lg,
                                    bc(rowb[:, GRP + 36 * layer:GRP + 36 * layer + 36].unsqueeze(1), [P, nt, 36]), ALU.add))
                L(dve.tensor_reduce(mg, lg[:, :, 0:NG], AX_X, ALU.max))
                dve.tensor_tensor(gx, lg[:, :, 0:NG], w3(mg, NG), ALU.subtract).then_inc(dv, 1)
                L(dve.tensor_tensor(gq, lg[:, :, 0:NG], w3(mg, NG), ALU.is_equal))
                L(dve.tensor_tensor(gq, gq, bc(iof[:, NE - NG:NE].unsqueeze(1), [P, nt, NG]), ALU.mult))
                L(dve.tensor_reduce(t1, gq, AX_X, ALU.max))
                L(dve.tensor_tensor(gq, gq, w3(t1, NG), ALU.is_equal))
                L(dve.tensor_scalar(gq, gq, -NEG, NEG, ALU.mult, ALU.add))
                for g in range(NG):
                    L(dve.tensor_tensor(el[:, :, NPG * g:NPG * g + NPG], lg[:, :, NG + NPG * g:NG + NPG * g + NPG],
                                        w3(gq[:, :, g], NPG), ALU.add))

                def top(m, oh):
                    L(dve.tensor_reduce(m, el, AX_X, ALU.max))
                    L(dve.tensor_tensor(eq, el, w3(m, NE), ALU.is_equal))
                    L(dve.tensor_tensor(eq, eq, bc(key32.unsqueeze(1), [P, nt, NE]), ALU.mult))
                    L(dve.tensor_reduce(t1, eq, AX_X, ALU.max))
                    L(dve.tensor_tensor(oh, eq, w3(t1, NE), ALU.is_equal))

                top(m1, oh1)
                L(dve.scalar_tensor_tensor(out=el, in0=oh1, scalar=4 * NEG, in1=el, op0=ALU.mult, op1=ALU.add))
                top(m2, oh2)
                dve.tensor_tensor(e2, m2, m1, ALU.subtract).then_inc(dv, 1)
                dve.tensor_tensor(cnt, oh1, oh2, ALU.add).then_inc(cn, 1)
                dve.wait_ge(ac, 1)
                L(dve.tensor_reduce(gs, gx, AX_X, ALU.add))
                dve.wait_ge(ac, 2)
                L(dve.tensor_scalar(r, e2, 1.0, None, ALU.add))
                L(dve.tensor_tensor(r, r, gs, ALU.mult))
                L(dve.reciprocal(gat[:, 0, 0:nt], r))
                L(dve.tensor_tensor(gat[:, 1, 0:nt], gat[:, 0, 0:nt], e2, ALU.mult))
                dve.wait_ge(pm, 1)
                dve.tensor_copy(ncol[0:NE, :], bank[2][0:NE, 0:1]).then_inc(nbd, 1)
                dve.wait_ge(nbd, 1)
                dve.tensor_scalar(tmp[0:NE, 0, 0:NBMAX - 1], iof[0:NE, NE:NE + NBMAX - 1], ncol[0:NE, :], 1.0,
                                  ALU.is_lt, ALU.add, accum_out=nb[0:NE, :]).then_inc(nbd, 1)
                L(dve.tensor_copy(rk.rearrange("p t n -> p (t n)"), bank[1][:, 0:nt * NE]))
                L(dve.tensor_copy(tot.rearrange("p t n -> p (t n)"), bank[1][:, 128:128 + nt * NE]))
                for j in range(1, nt):
                    L(dve.tensor_tensor(rk[:, j, :], rk[:, j, :], tot[:, j - 1, :], ALU.add))
                    if j + 1 < nt:
                        L(dve.tensor_tensor(tot[:, j, :], tot[:, j, :], tot[:, j - 1, :], ALU.add))
                dve.wait_ge(tbm, 1)
                dve.tensor_copy(tab[0:1, :], bank[3][0:1, 0:2 * NE + 1]).then_inc(tbd, 1)
                L(dve.tensor_scalar(base, bank[3][:, NE:2 * NE], float(B), None, ALU.mult))
                L(dve.tensor_tensor(rk, rk, bc(base.unsqueeze(1), [P, nt, NE]), ALU.add))
                for o, oh in enumerate((oh1, oh2)):
                    L(dve.tensor_tensor(tmp, rk, oh, ALU.mult))
                    L(dve.tensor_reduce(t2, tmp, AX_X, ALU.add))
                    dve.tensor_copy(pos[:, o, 0:nt], t2).then_inc(pd, 1)
                    dve.wait_ge(pd, o + 1)

            @block.gpsimd
            def _(pool):
                for o in range(2):
                    pool.wait_ge(pd, o + 1)
                    for j in range(nt):
                        pool.wait_ge(re, 2 * j + 2)
                        pool.indirect_dma_start(
                            out=xs, out_offset=bass.IndirectOffsetOnAxis(ap=pos[:, o, j:j + 1].bitcast(U32), axis=0),
                            in_=rows[j], in_offset=None).then_inc(sca, 16)
                pool.wait_ge(sca, 32 * nt)

    N_OF = [len(range(s, NE, 3)) for s in range(3)]

    PIECES = [(0, 0), (1, 0), (2, 16), (3, 16), (4, 32), (5, 32)]
    GATE_UP, DOWN = PIECES[:4], PIECES[4:]

    def load_expert(eng, layer, e, s, i, pieces=PIECES, down_is_free=lambda: None):
        gsrc = e_w_gu[layer].rearrange("e (k p) n -> p e k n", p=P)
        dsrc = e_w_dn[layer].rearrange("e (k p) n -> p e k n", p=P)
        for piece, count in pieces:
            ks = slice(2 * (piece % 4), 2 * (piece % 4) + 2)
            if count:
                eng.wait_ge(gu_loaded[s][piece % 2], 32 * i + count)
            if piece == 4:
                down_is_free()
            if piece < 4:
                eng.dma_start(gu_w[s][:, ks, :].unsqueeze(1), gsrc[:, bass.ds(e, 1), ks, :]).then_inc(gu_loaded[s][piece % 2], 16)
            else:
                eng.dma_start(dn_w[s][:, ks, :].unsqueeze(1), dsrc[:, bass.ds(e, 1), ks, :]).then_inc(dn_loaded[s][piece % 2], 16)

    @phase
    def experts(layer):
        a0 = PLACE["x"]
        xr = region(a0, 256)
        xT = region(a0 + 256, 256)
        sg, av, aT = (region(a0 + 512 + i * P, P) for i in range(3))
        yb = region(a0 + 1024, 256)
        xl, xt_t, xt_c, gu_mm, si_, a_, at_t, at_c, dn_mm, yc, yst = (sem(f"moe{layer}_{n}") for n in (
            "rows", "rows_turned", "columns", "gate_up", "silu", "hidden", "hidden_turned", "hidden_columns",
            "down", "copied", "stored"))
        quarters = lambda dram, t: dram[bass.ds(t * B, B), :].rearrange("t (c n) -> c t n", c=4)
        before_layer = [layer * n for n in N_OF]

        def blocks_of(eng, e):
            return (eng.value_load(tab[0:1, bass.ds(e, 1)], min_val=1, max_val=NBMAX),
                    eng.value_load(tab[0:1, bass.ds(e + NE, 1)], min_val=0, max_val=TMAX - 1))

        def total(eng):
            return eng.value_load(tab[0:1, 2 * NE:2 * NE + 1], min_val=NE, max_val=TMAX)

        with nc.Block() as block:
            @block.sync
            def _(sp):
                def refill(e, s, i):
                    nb, t0 = blocks_of(sp, e - 3)
                    sp.wait_ge(gu_mm, t0 + nb)
                    load_expert(sp, layer, e, s, i + before_layer[s],
                                down_is_free=lambda: sp.wait_ge(dn_mm, t0 + nb))

                with sp.Fori(1, NE // 3) as i:
                    for s in range(3):
                        refill(i * 3 + s, s, i)
                for s in range(NE % 3):
                    refill(NE // 3 * 3 + s, s, NE // 3)

            @block.gpsimd
            def _(pool):
                def load(t):
                    pool.dma_start(xr, quarters(xs, t)).then_inc(xl, 16)

                load(0)
                n = total(pool)
                with pool.Fori(1, n + 1) as t:
                    pool.wait_ge(xt_t, t)
                    load(t)
                pool.wait_ge(xl, (n + 1) * 16)

            @block.tensor
            def _(pe):
                def turn_rows(t):
                    pe.wait_ge(xl, (t + 1) * 16)
                    for hf in range(2):
                        last = pe.transpose(bank[0][:, hf * P:(hf + 1) * P], xr[:, hf * P:(hf + 1) * P], ident[:])
                    last.then_inc(xt_t, 1)

                def one_block(t, s, i):
                    pe.wait_ge(xt_c, t + 1)
                    for b in range(2):
                        pe.wait_ge(gu_loaded[s][b], (i + 1) * 32)
                    for k in range(KT):
                        w = gu_w[s][:, k, :].rearrange("p (h n) -> p h n", h=2)
                        lhs = xT[:, (k % 2) * P + (k // 2) * B:(k % 2) * P + (k // 2) * B + B]
                        for q in range(4):
                            last = pe.matmul(bank[1][32 * q:32 * q + 32, 0:256], lhs, w[:, :, q * P:(q + 1) * P],
                                             start=(k == 0), stop=(k == KT - 1), skip_group_check=True)
                    last.then_inc(gu_mm, 1)
                    turn_rows(t + 1)
                    pe.wait_ge(a_, t + 1)
                    pe.transpose(bank[2][:, 0:P], av, ident[:]).then_inc(at_t, 1)
                    pe.wait_ge(at_c, t + 1)
                    for b in range(2):
                        pe.wait_ge(dn_loaded[s][b], (i + 1) * 16)
                    pe.wait_ge(yc, t + 1)
                    for f in range(DE // P):
                        for q in range(4):
                            last = pe.matmul(bank[3][32 * q:32 * q + 32, 0:256], aT[:, f * B:(f + 1) * B],
                                             dn_w[s][:, f, q * 256:(q + 1) * 256], start=(f == 0), stop=(f == DE // P - 1),
                                             skip_group_check=True)
                    last.then_inc(dn_mm, 1)

                def expert(e, s, i):
                    nb, t0 = blocks_of(pe, e)
                    with pe.Fori(0, nb) as j:
                        one_block(t0 + j, s, i + before_layer[s])

                turn_rows(0)
                with pe.Fori(0, NE // 3) as i:
                    for s in range(3):
                        expert(i * 3 + s, s, i)
                for s in range(NE % 3):
                    expert(NE // 3 * 3 + s, s, NE // 3)

            @block.vector
            def _(dve):
                def columns(t):
                    dve.wait_ge(xt_t, t + 1)
                    dve.tensor_copy(xT, bank[0][:, 0:256]).then_inc(xt_c, 1)

                n = total(dve)
                columns(0)
                with dve.Fori(0, n) as t:
                    dve.wait_ge(si_, t + 1)
                    dve.tensor_tensor(av, sg, bank[1][:, P:2 * P], ALU.mult).then_inc(a_, 1)
                    columns(t + 1)
                    dve.wait_ge(at_t, t + 1)
                    dve.tensor_copy(aT, bank[2][:, 0:P]).then_inc(at_c, 1)

            @block.scalar
            def _(act):
                act.activation(yb[:, 0:1], eps[:], ACT.Copy).then_inc(yc, 1)
                act.dma_start(tabd[layer:layer + 1, :], tab[0:1, :]).then_inc(yst, 16)
                n = total(act)
                with act.Fori(0, n) as t:
                    act.wait_ge(gu_mm, t + 1)
                    act.activation(sg, bank[1][:, 0:P], ACT.Silu).then_inc(si_, 1)
                    act.wait_ge(dn_mm, t + 1)
                    act.wait_ge(yst, (t + 1) * 16)
                    act.activation(yb, bank[3][:, 0:256], ACT.Copy).then_inc(yc, 1)
                    act.wait_ge(yc, t + 2)
                    act.dma_start(quarters(ys, t), yb).then_inc(yst, 16)
                act.wait_ge(yst, (n + 1) * 16)
                act.activation(sg[:, 0:1], eps[:], ACT.Copy).then_inc(yc, 1)

    @phase
    def combine(layer, tiles, extra_sync=None):
        nt = len(tiles)
        streams = [0, 1] if nt == 4 else [1]
        Y = region(SLOT, 2 * nt, D)
        gm, ge, chain, xo, st = (sem(f"comb{layer}_{n}") for n in ("gate_mm", "gate", "chain", "added", "stored"))
        yl = [sem(f"comb{layer}_rows{j}") for j in range(nt)]
        fh = sem(f"comb{layer}_first_half")
        squares, std = sem(f"comb{layer}_squares"), sem(f"comb{layer}_std")
        with nc.Block() as block:
            @block.gpsimd
            def _(pool):
                for j in range(nt):
                    for o in range(2):
                        pool.indirect_dma_start(
                            out=Y[:, 2 * j + o, :], out_offset=None, in_=ys[0:TMAX * B, :],
                            in_offset=bass.IndirectOffsetOnAxis(ap=pos[:, o, j:j + 1].bitcast(U32), axis=0)).then_inc(yl[j], 16)

            @block.tensor
            def _(pe):
                gate_rows(pe, None, layer, 5, streams, gm, ge)

            @block.scalar
            def _(act):
                gate_rows(None, act, layer, 5, streams, gm, ge)

                def first_half(j):
                    act.wait_ge(yl[j], 32)
                    act.activation(Y[:, 2 * j, :], Y[:, 2 * j, :], ACT.Copy, scale=gat[:, 0, j:j + 1]).then_inc(fh, 1)

                first_half(0)
                for j, t in enumerate(tiles):
                    if j + 1 < nt:
                        first_half(j + 1)
                    if not layer:
                        act.wait_ge(xo, j + 1)
                        row_squares(act, j, t, S1[:, 0, :], squares)
                if not layer:
                    row_roots(act, nt, squares, std)

            @block.vector
            def _(dve):
                ch = Chain(chain)
                for j, t in enumerate(tiles):
                    dve.wait_ge(fh, j + 1)
                    dve.wait_ge(yl[j], 32)
                    a, b = Y[:, 2 * j, :], Y[:, 2 * j + 1, :]
                    ch.link(dve, dve.scalar_tensor_tensor(out=a, in0=b, scalar=gat[:, 1, j:j + 1], in1=a, op0=ALU.mult, op1=ALU.add))
                    dve.wait_ge(ge, 2 * (streams.index(t // 2) + 1))
                    ch.link(dve, dve.tensor_tensor(a, a, G[:, t // 2, :], ALU.mult))
                    dve.tensor_tensor(X[:, t, :], X[:, t, :], a, ALU.add).then_inc(xo, 1)
                if not layer:
                    row_inverses(dve, nt, std)

            @block.sync
            def _(sp):
                if extra_sync:
                    for j in range(nt):
                        sp.wait_ge(yl[j], 32)
                    extra_sync(sp)
                if layer:
                    for j, t in enumerate(tiles):
                        sp.wait_ge(xo, j + 1)
                        sp.dma_start(out[0, (t - 2) * P:(t - 1) * P, :], X[:, t, :]).then_inc(st, 16)
                    sp.wait_ge(st, 16 * nt)

    kT = region(SLOT, DH, TOK)
    V1 = region(SLOT + 4096, TILES, D)
    qT = region(SLOT + GU, DH, NLAT)
    A1 = region(SLOT + GU + 2048, 2, D)

    @phase
    def diff_project():
        tabs = MASK[:].rearrange("p a b -> p (a b)")
        cs = S2[:, 0, 0:256].rearrange("p (t w n) -> p t w n", t=TILES, w=2)
        Ck, Sk, Cq, Sq = (tabs[:, a:a + n * DDH].rearrange("p (t a h f) -> p t a h f", t=n, a=2, h=2)
                          for a, n in ((0, 4), (256, 4), (512, 2), (640, 2)))
        ssd, std, rstd = small[:, 96:104], small[:, 104:112], small[:, 112:120]
        sqb, xnb, t1b, t2b = S1[:, 0, 0:HALF], S1[:, 0, HALF:D], S1[:, 1, 0:HALF], S1[:, 1, HALF:D]
        kqb = [S2[:, 0, 256:256 + HALF], S2[:, 1, 0:HALF]]
        unit, ev, rp, sqs, st, xo, tr, te, chain = (sem(f"dproj_{n}") for n in (
            "unit", "evacuated", "rope", "squares", "std", "rows", "turned", "columns", "chain"))
        units = []
        for cidx in D_ORDER:
            kind = "qkv"[cidx // 2]
            for t in (LAT if kind == "q" else ALL):
                units.append((cidx, kind, cidx % 2, t))
        nqk = sum(u[1] != "v" for u in units)
        split = sem("dproj_cut")
        evv = sem("dproj_values_copied")
        CUT_ELSEWHERE = 3
        hi_cut = sem("dproj_high_cut")
        high = [place[to] for to in D_HIGH]
        last_of = [max(n for n, u in enumerate(units) if u[0] == cidx) for cidx in D_ORDER]
        plan = []
        for jc, cidx in enumerate(D_ORDER):
            mine = [n for n, u in enumerate(units) if u[0] == cidx]
            ada = [AT[key] for key in D_ADA[jc]]
            plan.append(("unit", mine[0]))
            rest = mine[1:]
            for m in ada:
                plan.append(("mul", m))
                if rest:
                    plan.append(("unit", rest.pop(0)))
                plan.append(("turn", m))
            plan += [("unit", r) for r in rest]
        multiplied.update({AT[("d_in", u[0])]: (unit, n + 1) for n, u in enumerate(units)})

        def cut(eng, j, qs):
            cut_quarters(eng, AT[("d_in", D_ORDER[j])], high[j], [(q, 4 * j + q) for q in qs],
                         (unit, last_of[j - 2] + 1) if j >= 2 else None, split)

        with nc.Block() as block:
            @block.sync
            def _(sp):
                sp.dma_start(cs, rope).then_inc(rp, 16)
                for n in range(AT[("d_in", 2)] + COMBINE_CHUNKS, AT[("d_out", 0)]):
                    load_chunk(sp, n)

            @block.gpsimd
            def _(pool):
                pool.wait_ge(split, 8 * CUT_ELSEWHERE)
                for j in range(CUT_ELSEWHERE, len(D_ORDER)):
                    full = place[STREAM_TO[AT[("d_in", D_ORDER[j])]]]
                    for q in range(4):
                        pool.wait_ge(hi_cut, 4 * (j - CUT_ELSEWHERE) + q + 1)
                        ks = slice(2 * q, 2 * q + 2)
                        cut_low(pool, full[:, ks, :], high[j][:, ks, :]).then_inc(split, 2)

            @block.tensor
            def _(pe):
                def turn(n):
                    pe.wait_ge(xo, n + 1)
                    if n:
                        pe.wait_ge(te, n)
                    for q in range(4):
                        last = pe.transpose(bank[5][:, q * P:(q + 1) * P], kqb[n % 2][:, q * P:(q + 1) * P], ident[:])
                    last.then_inc(tr, 1)

                turned = 0
                for what, n in plan:
                    if what == "unit":
                        cidx, kind, hf, t = units[n]
                        jc = D_ORDER.index(cidx)
                        w, wh = place[STREAM_TO[AT[("d_in", cidx)]]], high[jc]
                        if n - 4 >= nqk:
                            pe.wait_ge(evv, n - 3 - nqk)
                        elif n >= 4:
                            pe.wait_ge(ev, n - 3)
                        ts = slice(t * P, (t + 1) * P)
                        for k in range(KT):
                            if k % 2 == 0:
                                pe.wait_ge(split, 8 * jc + k + 2)
                            last = multiply3(pe, bank[n % 4][:], (hT[:, k, ts], hL[:, k, ts]), (wh[:, k, :], w[:, k, :]), k == 0, k == KT - 1)
                        last.then_inc(unit, 1)
                        while turned < min(n - 1, nqk):
                            turn(turned)
                            turned += 1
                    elif what == "mul":
                        ada_multiply(pe, n)
                    else:
                        ada_turn(pe, n)

            @block.scalar
            def _(act):
                def columns(n):
                    cidx, kind, hf, t = units[n]
                    act.wait_ge(tr, n + 1)
                    src = bank[5][:].rearrange("p (h n) -> p h n", h=4)
                    dst = kT[:, 4 * hf:4 * hf + 4, t * P:(t + 1) * P] if kind == "k" else qT[:, 4 * hf:4 * hf + 4, (t - 2) * P:(t - 1) * P]
                    act.activation(dst, src, ACT.Copy).then_inc(te, 1)

                def high_parts(j):
                    full = chunk(act, AT[("d_in", D_ORDER[j])])
                    act.wait_ge(unit, last_of[j - 2] + 1)
                    for q in range(4):
                        ks = slice(2 * q, 2 * q + 2)
                        act.activation(rounded(high[j][:, ks, :]), full[:, ks, :], ACT.Copy).then_inc(hi_cut, 1)

                for n, (cidx, kind, hf, t) in enumerate(units):
                    act.wait_ge(unit, n + 1)
                    if kind == "v":
                        act.activation(V1[:, t, hf * HALF:(hf + 1) * HALF], bank[n % 4][:], ACT.Copy).then_inc(evv, 1)
                        if n - 2 < nqk:
                            columns(n - 2)
                    else:
                        if n:
                            act.wait_ge(sqs, 2 * n)
                        act.activation(sqb, bank[n % 4][:], ACT.Square).then_inc(sqs, 1)
                        act.wait_ge(st, 2 * n + 1)
                        act.activation(std, ssd, ACT.Sqrt, bias=eps[:], scale=1.0 / DDH).then_inc(st, 1)
                        if n >= 2:
                            columns(n - 2)
                    j = D_ORDER.index(cidx)
                    if CUT_ELSEWHERE <= j + 1 < len(D_ORDER) and n == last_of[j - 1] + 1:
                        high_parts(j + 1)

            @block.vector
            def _(dve):
                ch = Chain(chain)
                L = lambda ins: ch.link(dve, ins)
                cut(dve, 0, range(4))
                dve.wait_ge(rp, 16)
                for Ct, St, gcol, tiles in ((Ck, Sk, KG, ALL), (Cq, Sq, QG, LAT)):
                    gv = rowb[:, gcol:gcol + DDH].rearrange("p (a h f) -> p a h f", a=2, h=2)
                    for i, t in enumerate(tiles):
                        co = cs[:, t, 0, :].rearrange("p (a f) -> p a f", a=2)
                        so = cs[:, t, 1, :].rearrange("p (a f) -> p a f", a=2)
                        for h in range(2):
                            L(dve.tensor_tensor(Ct[:, i, :, h, :], gv[:, :, h, :], co, ALU.mult))
                            L(dve.scalar_tensor_tensor(out=St[:, i, :, h, :], in0=gv[:, :, 1 - h, :], scalar=(-1.0 if h == 0 else 1.0),
                                                       in1=so, op0=ALU.mult, op1=ALU.mult))

                def rows(n):
                    cidx, kind, hf, t = units[n]
                    Ct, St = (Ck[:, t], Sk[:, t]) if kind == "k" else (Cq[:, t - 2], Sq[:, t - 2])
                    dve.wait_ge(sqs, 2 * n + 1)
                    if n:
                        dve.wait_ge(st, 2 * n)
                    dve.tensor_reduce(ssd, sqb.rearrange("p (g n) -> p g n", g=8), AX_X, ALU.add).then_inc(st, 1)
                    dve.wait_ge(st, 2 * n + 2)
                    dve.reciprocal(rstd, std).then_inc(sqs, 1)
                    dve.wait_ge(sqs, 2 * n + 2)
                    g8 = lambda v: v.rearrange("p (g n) -> p g n", g=8)
                    dve.tensor_tensor(g8(xnb), g8(bank[n % 4][:]), bc(rstd.unsqueeze(2), [P, 8, DDH]), ALU.mult).then_inc(ev, 1)
                    dve.wait_ge(ev, n + 1)
                    L(dve.tensor_tensor(g8(t1b), g8(xnb), bc(Ct.rearrange("p a h f -> p (a h f)").unsqueeze(1), [P, 8, DDH]), ALU.mult))
                    v = lambda b, h: b.rearrange("p (g a h f) -> p g a h f", g=8, a=2, h=2)[:, :, :, h, :]
                    for h in range(2):
                        L(dve.tensor_tensor(v(t2b, h), v(xnb, 1 - h), bc(St[:, :, h, :].unsqueeze(1), [P, 8, 2, 16]), ALU.mult))
                    if n >= 2:
                        dve.wait_ge(tr, n - 1)
                    dve.tensor_tensor(kqb[n % 2], t1b, t2b, ALU.add).then_inc(xo, 1)

                for what, n in plan:
                    if what == "unit":
                        if n < nqk:
                            rows(n)
                        jc = D_ORDER.index(units[n][0])
                        z = n - (last_of[jc - 1] + 1 if jc else 0)
                        if jc + 1 < CUT_ELSEWHERE and z < 3:
                            cut(dve, jc + 1, ((0,), (1,), (2, 3))[z])
                    elif what == "mul":
                        ada_copy(dve, n)
                    else:
                        ada_finish(dve, n)

    @phase
    def diff_attend():
        lamb = small[:, 96:104]
        E = [S1[:, b, :].rearrange("p (m n) -> p m n", m=2) for b in range(2)]
        PT = [S2[:, b, 0:HALF] for b in range(2)]
        stat = small[:, 128:256].rearrange("p (i n) -> p i n", i=16)
        ss, std, rstd = small[:, 256:272], small[:, 272:288], small[:, 288:304]
        s_mm, mx, ex, pr, tr, pt, pv, oc, fin, chain, lam_s, lam_a = (sem(f"datt_{n}") for n in (
            "scores", "max", "exp", "weights", "turned", "copied", "heads", "out", "final", "chain", "lam", "lam_exp"))
        ITER = [(j, h) for j in range(2) for h in range(DH)]
        scale = DDH ** -0.5
        with nc.Block() as block:
            @block.sync
            def _(sp):
                load_chunk(sp, AT[("d_out", 0)])
                load_chunk(sp, AT[("d_out", 1)])
                load_expert(sp, 1, 0, 0, N_OF[0])

            @block.tensor
            def _(pe):
                def scores(i):
                    j, h = ITER[i]
                    if i >= 2:
                        pe.wait_ge(ex, 2 * (i - 1))
                    for m in range(2):
                        lo = DDH * m
                        last = pe.matmul(bank[2 * (i % 2) + m][:], qT[lo:lo + DDH, h, j * P:(j + 1) * P], kT[lo:lo + DDH, h, :],
                                         start=True, stop=True)
                    last.then_inc(s_mm, 1)

                def turn(i):
                    pe.wait_ge(pr, i + 1)
                    if i >= 2:
                        pe.wait_ge(pt, i - 1)
                    for s in range(4):
                        last = pe.transpose(bank[4 + i % 2][:, s * P:(s + 1) * P], E[i % 2][:, 1, s * P:(s + 1) * P], ident[:])
                    last.then_inc(tr, 1)

                def heads(i):
                    j, h = ITER[i]
                    pe.wait_ge(pt, i + 1)
                    if i >= 2:
                        pe.wait_ge(oc, i - 1)
                    for s in range(4):
                        last = pe.matmul(bank[6 + i % 2][:, 0:DDV], PT[i % 2][:, s * P:(s + 1) * P], V1[:, s, h * DDV:(h + 1) * DDV],
                                         start=(s == 0), stop=(s == 3))
                    last.then_inc(pv, 1)

                scores(0)
                scores(1)
                for i in range(16):
                    if i + 2 < 16:
                        scores(i + 2)
                    turn(i)
                    if i:
                        heads(i - 1)
                heads(15)

            @block.scalar
            def _(act):
                act.wait_ge(lam_s, 2)
                act.activation(lamb[:, 2:4], lamb[:, 0:2], ACT.Exp).then_inc(lam_a, 1)

                def exps(i):
                    act.wait_ge(mx, 2 * i + 2)
                    if i >= 2:
                        act.wait_ge(tr, i - 1)
                    for m in range(2):
                        act.activation(E[i % 2][:, m, :], bank[2 * (i % 2) + m][:], ACT.Exp, bias=stat[:, i, m:m + 1], scale=scale,
                                       accum_out=stat[:, i, 2 + m:3 + m]).then_inc(ex, 1)

                exps(0)
                for i in range(16):
                    if i + 1 < 16:
                        exps(i + 1)
                    act.wait_ge(tr, i + 1)
                    if i >= 2:
                        act.wait_ge(pv, i - 1)
                    act.activation(PT[i % 2], bank[4 + i % 2][:], ACT.Copy).then_inc(pt, 1)
                act.wait_ge(fin, 1)
                act.activation(std, ss, ACT.Sqrt, bias=eps[:], scale=1.0 / DDV).then_inc(fin, 1)

            @block.vector
            def _(dve):
                ch = Chain(chain)
                L = lambda ins: ch.link(dve, ins)
                for o in range(2):
                    a = LQ + 2 * DDH * o
                    dve.tensor_tensor_reduce(small[:, 320:384], rowb[:, a:a + DDH], rowb[:, a + DDH:a + 2 * DDH], 1.0, 0.0,
                                             ALU.mult, ALU.add, lamb[:, o:o + 1]).then_inc(lam_s, 1)
                    dve.wait_ge(lam_s, o + 1)

                def maxima(i):
                    dve.wait_ge(s_mm, i + 1)
                    for m in range(2):
                        L(dve.tensor_reduce(stat[:, i, 4 + m:5 + m], bank[2 * (i % 2) + m][:], AX_X, ALU.max))
                    dve.tensor_scalar(stat[:, i, 0:2], stat[:, i, 4:6], -scale, None, ALU.mult).then_inc(mx, 2)

                maxima(0)
                maxima(1)
                dve.wait_ge(lam_a, 1)
                L(dve.tensor_tensor(lamb[:, 4:5], lamb[:, 3:4], lamb[:, 2:3], ALU.subtract))
                L(dve.tensor_scalar(lamb[:, 5:6], lamb[:, 4:5], LAMBDA_INIT, None, ALU.subtract))

                def head_out(i):
                    j, h = ITER[i]
                    dve.wait_ge(pv, i + 1)
                    dve.tensor_copy(A1[:, j, h * DDV:(h + 1) * DDV], bank[6 + i % 2][:, 0:DDV]).then_inc(oc, 1)

                def squares(j):
                    dve.wait_ge(oc, 8 * j + 8)
                    tmp = region(PLACE["x"], D)
                    L(dve.tensor_tensor(tmp, A1[:, j, :], A1[:, j, :], ALU.mult))
                    L(dve.tensor_reduce(ss[:, 8 * j:8 * j + 8], tmp.rearrange("p (h n) -> p h n", h=8), AX_X, ALU.add))

                for i in range(16):
                    dve.wait_ge(ex, 2 * i + 2)
                    L(dve.reciprocal(stat[:, i, 6:8], stat[:, i, 2:4]))
                    L(dve.tensor_scalar(stat[:, i, 7:8], stat[:, i, 7:8], lamb[:, 5:6], None, ALU.mult))
                    e0, e1 = E[i % 2][:, 0, :], E[i % 2][:, 1, :]
                    L(dve.tensor_scalar(e0, e0, stat[:, i, 6:7], None, ALU.mult))
                    dve.scalar_tensor_tensor(out=e1, in0=e1, scalar=stat[:, i, 7:8], in1=e0, op0=ALU.mult, op1=ALU.add).then_inc(pr, 1)
                    if i + 2 < 16:
                        maxima(i + 2)
                    if i >= 2:
                        head_out(i - 2)
                    if i == 12:
                        squares(0)
                head_out(14)
                head_out(15)
                squares(1)
                dve.tensor_copy(small[:, 104:105], eps[:]).then_inc(fin, 1)
                dve.wait_ge(fin, 2)
                L(dve.reciprocal(rstd, std))
                for j in range(2):
                    v = A1[:, j, :].rearrange("p (h n) -> p h n", h=8)
                    L(dve.tensor_tensor(v, v, bc(rstd[:, 8 * j:8 * j + 8].unsqueeze(2), [P, 8, DDV]), ALU.mult))

    def under_output0(sp):
        load_expert(sp, 0, 0, 0, 0, GATE_UP)
        load_expert(sp, 0, 1, 1, 0, [(2, 0), (3, 0), (4, 16), (5, 16)])

    def under_norm0(sp):
        load_expert(sp, 0, 0, 0, 0, DOWN)
        load_expert(sp, 0, 1, 1, 0, [(0, 16), (1, 16)])

    def under_route0(sp):
        load_expert(sp, 0, 2, 2, 0)

    def first_chunks(sp):
        for n in range(AT[("d_in", 2)], AT[("d_in", 2)] + COMBINE_CHUNKS):
            load_chunk(sp, n)

    def under_output1(sp):
        load_expert(sp, 1, 1, 1, N_OF[1], GATE_UP)

    def under_norm1(sp):
        load_expert(sp, 1, 1, 1, N_OF[1], DOWN)
        load_expert(sp, 1, 2, 2, N_OF[2], GATE_UP[:2])

    def under_route1(sp):
        load_expert(sp, 1, 2, 2, N_OF[2], PIECES[2:])

    setup()
    norm(0, 0, ALL, hL, None, hT)
    mlstm_project()
    mlstm_attend()
    output(0, ALL, O, lambda k: vT[:, 2, OUTG + k:OUTG + k + 1], "m_out", under_output0)
    norm(0, 1, ALL, h2T, under_norm0)
    route(0, ALL, under_route0)
    experts(0)
    combine(0, ALL, first_chunks)
    norm(1, 0, ALL, hL, None, hT)
    diff_project()
    diff_attend()
    output(1, LAT, A1, lambda k: small[:, 28:29], "d_out", under_output1)
    norm(1, 1, LAT, h2T, under_norm1)
    route(1, LAT, under_route1)
    experts(1)
    combine(1, LAT)
    stack.close()


_INS = ["x", "c", "ctx", "c_ctx", "ada_w", "ada_b", "norm1_g", "norm2_g", "m_w_in", "m_conv_w", "m_conv_b", "m_gate_b",
        "m_out_g", "m_w_out", "d_w_in", "d_q_g", "d_k_g", "d_lq1", "d_lk1", "d_lq2", "d_lk2", "d_sub_g", "d_w_out",
        "r_grp_w", "r_grp_b", "r_exp_w", "r_exp_b", "e_w_gu", "e_w_dn"]
_OUT = (1, NLAT, D)


def rope_constants():
    import numpy as np
    grid_w, freqs = 64, DDH // 4
    inv = (np.float32(10000.0) ** (-np.arange(freqs, dtype=np.float32) / np.float32(freqs))).astype(np.float32)
    t = np.arange(NLAT)
    place = np.stack([t // grid_w, t % grid_w], -1).astype(np.float32)
    ang = (place[..., None] * inv).reshape(NLAT, 2 * freqs)
    cs = np.zeros((TOK, 2, 2 * freqs), np.float32)
    cs[:, 0] = 1.0
    cs[NCTX:, 0] = np.cos(ang)
    cs[NCTX:, 1] = np.sin(ang)
    return np.ascontiguousarray(cs.reshape(TILES, P, 2, 2 * freqs).transpose(1, 0, 2, 3))


def kernel(**inputs):
    import numpy as _np
    import concourse.bacc as _bacc
    from concourse import mybir as _mybir
    from concourse.bass_utils import run_bass_kernel_spmd as _run

    nc = _bacc.Bacc("TRN2", target_bir_lowering=False, num_devices=1, dynamic_dma_scratch_size=8192)
    arrays, args = {}, []
    given = {n: _np.ascontiguousarray(inputs[n]) for n in _INS}
    given["rope"] = rope_constants()
    for name, a in given.items():
        arrays[f"in_{name}_dram"] = a
        args.append(nc.dram_tensor(f"in_{name}_dram", a.shape, _mybir.dt.from_np(a.dtype), kind="ExternalInput").ap())
    out = nc.dram_tensor("out_0_dram", _OUT, _mybir.dt.float32, kind="ExternalOutput").ap()
    hybrid_backbone(nc, *args, out)
    r = _run(nc, [arrays], core_ids=[0])
    return r.results[0]["out_0_dram"]
```
